# Optimizing a Trainium2 kernel written in Bass

```python
import math
import jax, jax.numpy as jnp
from jax import lax
import numpy as np

D_MODEL = 1024
BATCH = 1
SEQ = 512
DEPTH = 1

GDN_HEADS = 8
GDN_HEAD_DIM = 128
GDN_WIDTH = GDN_HEADS * GDN_HEAD_DIM
SSD_HEADS = 16
SSD_HEAD_DIM = 64
SSD_WIDTH = SSD_HEADS * SSD_HEAD_DIM
SSD_GROUPS = 2
SSD_STATE = 128
BC_WIDTH = SSD_GROUPS * SSD_STATE
MIX_WIDTH = GDN_WIDTH + SSD_WIDTH
CONV_K = 7
CHUNK = 64
N_EXPERTS = 16
EXPERT_FF = 512
EC_FACTOR = 2
EPS = 1e-6
DT_MIN = 1e-3
DT_MAX = 0.1

CONV_CH = 3 * GDN_WIDTH + SSD_WIDTH + 2 * BC_WIDTH
GATE_CH = GDN_WIDTH + SSD_WIDTH
SCALAR_CH = 4 * GDN_HEADS + 2 * SSD_HEADS
PROJ_OUT = CONV_CH + GATE_CH + SCALAR_CH


F32 = jnp.float32

def rms_norm(x, w):
    xf = x.astype(F32)
    y = xf * lax.rsqrt(jnp.mean(xf * xf, axis=-1, keepdims=True) + EPS)
    return (y * w.astype(F32)).astype(x.dtype)

def l2_normalize(t):
    return t * lax.rsqrt(jnp.sum(t * t, axis=-1, keepdims=True) + EPS)

def centred_dwconv(x, w, b):
    pad = (CONV_K - 1) // 2
    L = x.shape[1]
    xp = jnp.pad(x, ((0, 0), (pad, pad), (0, 0)))
    out = xp[:, 0:L] * w[0]
    for tap in range(1, CONV_K):
        out = out + xp[:, tap:tap + L] * w[tap]
    return out + b

def flip_seq(t):
    return jnp.flip(t, axis=1)

def gated_delta_chunked(q, k, v, g, beta):
    Bsz, L, H, Dk = q.shape
    Dv = v.shape[-1]
    N = L // CHUNK

    def to_chunks(t):
        t = t.reshape((Bsz, N, CHUNK) + t.shape[2:])
        return jnp.swapaxes(t, 2, 3)

    q, k, v, g, beta = (to_chunks(t) for t in (q, k, v, g, beta))
    gc = jnp.cumsum(g, axis=-1)
    incl = jnp.tril(jnp.ones((CHUNK, CHUNK), bool))
    strict = jnp.tril(jnp.ones((CHUNK, CHUNK), bool), k=-1)
    decay = jnp.exp(jnp.where(incl, gc[..., :, None] - gc[..., None, :], -jnp.inf))
    kk = jnp.einsum('bnhid,bnhjd->bnhij', k, k)
    A = jnp.where(strict, beta[..., :, None] * kk * decay, 0.0)
    rhs = jnp.concatenate([v * beta[..., None], k * (beta * jnp.exp(gc))[..., None]], axis=-1)
    sol = lax.linalg.triangular_solve(A, rhs, left_side=True, lower=True, unit_diagonal=True)
    u_v, w_k = sol[..., :Dv], sol[..., Dv:]
    qk = jnp.einsum('bnhid,bnhjd->bnhij', q, k) * decay
    q_dec = q * jnp.exp(gc)[..., None]
    g_last = gc[..., -1]
    k_dec = k * jnp.exp(g_last[..., None] - gc)[..., None]

    def step(S, inp):
        u_c, w_c, qk_c, qd_c, kd_c, gl_c = inp
        u_new = u_c - jnp.einsum('bhik,bhkv->bhiv', w_c, S)
        o = jnp.einsum('bhik,bhkv->bhiv', qd_c, S) + jnp.einsum('bhij,bhjv->bhiv', qk_c, u_new)
        S = S * jnp.exp(gl_c)[..., None, None] + jnp.einsum('bhjk,bhjv->bhkv', kd_c, u_new)
        return S, o

    xs = tuple(jnp.moveaxis(t, 1, 0) for t in (u_v, w_k, qk, q_dec, k_dec, g_last))
    S0 = jnp.zeros((Bsz, H, Dk, Dv), F32)
    _, o = lax.scan(step, S0, xs)
    return jnp.transpose(o, (1, 0, 3, 2, 4)).reshape(Bsz, L, H, Dv)

def ssd_chunked(x, dt, A, Bm, Cm):
    Bsz, L, H, P = x.shape
    G, Ns = Bm.shape[2], Bm.shape[3]
    Hg = H // G
    N = L // CHUNK
    x = x.reshape(Bsz, N, CHUNK, G, Hg, P)
    dt = dt.reshape(Bsz, N, CHUNK, G, Hg)
    Bm = Bm.reshape(Bsz, N, CHUNK, G, Ns)
    Cm = Cm.reshape(Bsz, N, CHUNK, G, Ns)
    cs = jnp.cumsum(dt * A.reshape(G, Hg), axis=2)
    incl = jnp.tril(jnp.ones((CHUNK, CHUNK), bool))[:, :, None, None]
    Lmat = jnp.exp(jnp.where(incl, cs[:, :, :, None] - cs[:, :, None, :], -jnp.inf))
    cb = jnp.einsum('bnigs,bnjgs->bnijg', Cm, Bm)
    xdt = x * dt[..., None]
    y_intra = jnp.einsum('bnijgh,bnjghp->bnighp', cb[..., None] * Lmat, xdt)
    cs_last = cs[:, :, -1]
    w_state = jnp.exp(cs_last[:, :, None] - cs)
    chunk_states = jnp.einsum('bnjgs,bnjghp->bnghsp', Bm, xdt * w_state[..., None])

    def step(hst, inp):
        st, dec, c_c, ecs_c = inp
        y = jnp.einsum('bigs,bghsp->bighp', c_c, hst) * ecs_c[..., None]
        hst = hst * jnp.exp(dec)[..., None, None] + st
        return hst, y

    xs = tuple(jnp.moveaxis(t, 1, 0) for t in (chunk_states, cs_last, Cm, jnp.exp(cs)))
    h0 = jnp.zeros((Bsz, G, Hg, Ns, P), F32)
    _, y_inter = lax.scan(step, h0, xs)
    y = y_intra + jnp.moveaxis(y_inter, 0, 1)
    return y.reshape(Bsz, L, H, P)

def hybrid_mixer(n, w_in, conv_w, conv_b, gdn_A_log, gdn_dt_bias, gdn_norm_w,
                 ssd_A_log, ssd_dt_bias, ssd_D, ssd_norm_w, w_out):
    Bsz, L, _ = n.shape
    proj = jnp.einsum('bld,dp->blp', n, w_in)
    conv_in, gates, scal = jnp.split(proj, [CONV_CH, CONV_CH + GATE_CH], axis=-1)
    c = jax.nn.silu(centred_dwconv(conv_in, conv_w, conv_b)).astype(F32)
    q, k, v, xs, Bm, Cm = jnp.split(
        c, [GDN_WIDTH, 2 * GDN_WIDTH, 3 * GDN_WIDTH, 3 * GDN_WIDTH + SSD_WIDTH,
            3 * GDN_WIDTH + SSD_WIDTH + BC_WIDTH], axis=-1)
    g_gate, z = jnp.split(gates.astype(F32), [GDN_WIDTH], axis=-1)
    gh, sh = GDN_HEADS, SSD_HEADS
    b_f, b_b, a_f, a_b, dt_f, dt_b = jnp.split(
        scal.astype(F32), [gh, 2 * gh, 3 * gh, 4 * gh, 4 * gh + sh], axis=-1)

    q = l2_normalize(q.reshape(Bsz, L, gh, GDN_HEAD_DIM)) * (GDN_HEAD_DIM ** -0.5)
    k = l2_normalize(k.reshape(Bsz, L, gh, GDN_HEAD_DIM))
    v = v.reshape(Bsz, L, gh, GDN_HEAD_DIM)
    gA = gdn_A_log.astype(F32)
    gB = gdn_dt_bias.astype(F32)
    g_fw = -jnp.exp(gA[0]) * jax.nn.softplus(a_f + gB[0])
    g_bw = -jnp.exp(gA[1]) * jax.nn.softplus(a_b + gB[1])
    o_fw = gated_delta_chunked(q, k, v, g_fw, jax.nn.sigmoid(b_f))
    o_bw = flip_seq(gated_delta_chunked(flip_seq(q), flip_seq(k), flip_seq(v),
                                        flip_seq(g_bw), flip_seq(jax.nn.sigmoid(b_b))))
    o_gdn = rms_norm(o_fw + o_bw, gdn_norm_w) * jax.nn.silu(g_gate.reshape(Bsz, L, gh, GDN_HEAD_DIM))
    o_gdn = o_gdn.reshape(Bsz, L, GDN_WIDTH)

    x_ssd = xs.reshape(Bsz, L, sh, SSD_HEAD_DIM)
    Bm = Bm.reshape(Bsz, L, SSD_GROUPS, SSD_STATE)
    Cm = Cm.reshape(Bsz, L, SSD_GROUPS, SSD_STATE)
    sA = -jnp.exp(ssd_A_log.astype(F32))
    sB = ssd_dt_bias.astype(F32)
    dt_fw = jax.nn.softplus(dt_f + sB[0])
    dt_bw = jax.nn.softplus(dt_b + sB[1])
    y_fw = ssd_chunked(x_ssd, dt_fw, sA[0], Bm, Cm)
    y_bw = flip_seq(ssd_chunked(flip_seq(x_ssd), flip_seq(dt_bw), sA[1], flip_seq(Bm), flip_seq(Cm)))
    y = y_fw + y_bw + ssd_D.astype(F32)[:, None] * x_ssd
    y = y.reshape(Bsz, L, SSD_WIDTH) * jax.nn.silu(z)
    y = rms_norm(y.reshape(Bsz, L, SSD_GROUPS, SSD_WIDTH // SSD_GROUPS),
                 ssd_norm_w.reshape(SSD_GROUPS, SSD_WIDTH // SSD_GROUPS)).reshape(Bsz, L, SSD_WIDTH)

    mixed = jnp.concatenate([o_gdn, y], axis=-1).astype(n.dtype)
    return jnp.einsum('blm,md->bld', mixed, w_out)

def expert_choice_ffn(n, w_router, w_gate, w_up, w_down):
    Bsz, L, D = n.shape
    cap = EC_FACTOR * L // N_EXPERTS
    logits = jnp.einsum('bld,de->ble', n, w_router).astype(F32)
    aff = jax.nn.softmax(logits, axis=-1)
    vals, idx = lax.top_k(jnp.swapaxes(aff, 1, 2), cap)
    xs = jax.vmap(lambda hb, ib: hb[ib])(n, idx)
    a = jnp.einsum('becd,edf->becf', xs, w_gate)
    u = jnp.einsum('becd,edf->becf', xs, w_up)
    y = jnp.einsum('becf,efd->becd', jax.nn.silu(a) * u, w_down) * vals[..., None].astype(n.dtype)
    return jax.vmap(lambda yb, ib: jnp.zeros((L, D), yb.dtype).at[ib.reshape(-1)].add(yb.reshape(-1, D)))(y, idx)

def _inv_softplus(t):
    return t + jnp.log(-jnp.expm1(-t))

def first_inputs(seed: int = 0) -> dict:
    key = jax.random.key(seed)
    ks = jax.random.split(key, 20)

    def normal(k, shape, scale):
        return jax.random.normal(k, shape, F32) * scale

    def gain(k, shape):
        return 1.0 + 0.02 * jax.random.normal(k, shape, F32)

    def dt_bias(k, shape):
        u = jax.random.uniform(k, shape, F32)
        dt = jnp.exp(u * (math.log(DT_MAX) - math.log(DT_MIN)) + math.log(DT_MIN))
        return _inv_softplus(dt)

    def a_log(k, shape):
        return jnp.log(jax.random.uniform(k, shape, F32, 1.0, 16.0))

    return {
        "x": jax.random.normal(ks[0], (BATCH, SEQ, D_MODEL), F32),
        "norm1_w": gain(ks[1], (DEPTH, D_MODEL)),
        "w_in": normal(ks[2], (DEPTH, D_MODEL, PROJ_OUT), D_MODEL ** -0.5),
        "conv_w": normal(ks[3], (DEPTH, CONV_K, CONV_CH), CONV_K ** -0.5),
        "conv_b": normal(ks[4], (DEPTH, CONV_CH), 0.01),
        "gdn_A_log": a_log(ks[5], (DEPTH, 2, GDN_HEADS)),
        "gdn_dt_bias": dt_bias(ks[6], (DEPTH, 2, GDN_HEADS)),
        "gdn_norm_w": gain(ks[7], (DEPTH, GDN_HEAD_DIM)),
        "ssd_A_log": a_log(ks[8], (DEPTH, 2, SSD_HEADS)),
        "ssd_dt_bias": dt_bias(ks[9], (DEPTH, 2, SSD_HEADS)),
        "ssd_D": gain(ks[10], (DEPTH, SSD_HEADS)),
        "ssd_norm_w": gain(ks[11], (DEPTH, SSD_WIDTH)),
        "w_out": normal(ks[12], (DEPTH, MIX_WIDTH, D_MODEL), MIX_WIDTH ** -0.5),
        "norm2_w": gain(ks[13], (DEPTH, D_MODEL)),
        "w_router": normal(ks[14], (DEPTH, D_MODEL, N_EXPERTS), D_MODEL ** -0.5),
        "w_gate": normal(ks[15], (DEPTH, N_EXPERTS, D_MODEL, EXPERT_FF), D_MODEL ** -0.5),
        "w_up": normal(ks[16], (DEPTH, N_EXPERTS, D_MODEL, EXPERT_FF), D_MODEL ** -0.5),
        "w_down": normal(ks[17], (DEPTH, N_EXPERTS, EXPERT_FF, D_MODEL), EXPERT_FF ** -0.5),
        "final_norm_w": gain(ks[18], (D_MODEL,)),
    }

def first_block(x, norm1_w, w_in, conv_w, conv_b, gdn_A_log, gdn_dt_bias, gdn_norm_w,
              ssd_A_log, ssd_dt_bias, ssd_D, ssd_norm_w, w_out, norm2_w, w_router,
              w_gate, w_up, w_down, final_norm_w):
    h = x
    for layer in range(DEPTH):
        h = h + hybrid_mixer(rms_norm(h, norm1_w[layer]), w_in[layer], conv_w[layer], conv_b[layer],
                             gdn_A_log[layer], gdn_dt_bias[layer], gdn_norm_w[layer],
                             ssd_A_log[layer], ssd_dt_bias[layer], ssd_D[layer], ssd_norm_w[layer],
                             w_out[layer])
        h = h + expert_choice_ffn(rms_norm(h, norm2_w[layer]), w_router[layer], w_gate[layer],
                                  w_up[layer], w_down[layer])
    return rms_norm(h, final_norm_w)


DEPTH_2 = 2

N_META = 16
HEAD_DIM = 64
N_Q_HEADS = 8
N_KV_HEADS = 2
GROUP = N_Q_HEADS // N_KV_HEADS
ATTN_WIDTH = N_Q_HEADS * HEAD_DIM
KV_WIDTH = N_KV_HEADS * HEAD_DIM
WINDOW = 128
BLOCK = 128
CONV_CH_2 = D_MODEL // 2
CONV_WIDTH = 31
N_BUCKETS = 32
MAX_DISTANCE = 128
D_FF = 2816
N_EXPERTS_2 = 8
TOP_K = 2
D_EXPERT = 1408
N_DENSE = (DEPTH_2 + 1) // 2
N_MOE = DEPTH_2 // 2
ALPHA = (2 * DEPTH_2) ** 0.25
BETA = (8 * DEPTH_2) ** -0.25
LN_EPS = 1e-5
Q_END = ATTN_WIDTH
K_END = Q_END + KV_WIDTH
V_END = K_END + KV_WIDTH
GLU_END = V_END + 2 * CONV_CH_2
GA_END = GLU_END + D_MODEL
GC_END = GA_END + D_MODEL
IN_WIDTH = GC_END


def layer_norm(x, g, b):
    xf = x.astype(jnp.float32)
    mu = jnp.mean(xf, -1, keepdims=True)
    var = jnp.mean(jnp.square(xf - mu), -1, keepdims=True)
    y = (xf - mu) * lax.rsqrt(var + LN_EPS) * g.astype(jnp.float32) + b.astype(jnp.float32)
    return y.astype(x.dtype)

def rel_bucket(dist):
    n = jnp.maximum(dist, 0)
    max_exact = N_BUCKETS // 2
    nf = jnp.maximum(n, 1).astype(jnp.float32)
    large = max_exact + (jnp.log(nf / max_exact) / math.log(MAX_DISTANCE / max_exact)
                         * (N_BUCKETS - max_exact)).astype(jnp.int32)
    large = jnp.minimum(large, N_BUCKETS - 1)
    return jnp.where(n < max_exact, n, large)

def head_bias(rel_bias, bucket):
    b = rel_bias.astype(jnp.float32)[bucket]
    b = jnp.moveaxis(b, -1, -3)
    return b.reshape(b.shape[:-3] + (N_KV_HEADS, GROUP) + b.shape[-2:])

def sink_softmax(s, sink):
    m = jnp.maximum(jnp.max(s, -1, keepdims=True), sink)
    p = jnp.exp(s - m)
    return p / (jnp.sum(p, -1, keepdims=True) + jnp.exp(sink - m))

def sliding_window_attention(q, k, v, sinks, rel_bias):
    B, L = q.shape[:2]
    S = L - N_META
    nb = S // BLOCK
    scale = HEAD_DIM ** -0.5
    sink = sinks.astype(jnp.float32).reshape(N_KV_HEADS, GROUP)[:, :, None, None]

    qm = q[:, :N_META].reshape(B, N_META, N_KV_HEADS, GROUP, HEAD_DIM)
    km, vm = k[:, :N_META], v[:, :N_META]

    pos_m = jnp.arange(N_META)
    dist_mm = pos_m[:, None] - pos_m[None, :]
    s_mm = jnp.einsum('bqhgd,bkhd->bhgqk', qm, km).astype(jnp.float32) * scale
    s_mm = s_mm + head_bias(rel_bias, rel_bucket(dist_mm))
    s_mm = jnp.where(dist_mm >= 0, s_mm, -jnp.inf)
    p_mm = sink_softmax(s_mm, sink).astype(v.dtype)
    o_m = jnp.einsum('bhgqk,bkhd->bqhgd', p_mm, vm).reshape(B, N_META, ATTN_WIDTH)

    qr = q[:, N_META:].reshape(B, nb, BLOCK, N_KV_HEADS, GROUP, HEAD_DIM)
    kr = k[:, N_META:].reshape(B, nb, BLOCK, N_KV_HEADS, HEAD_DIM)
    vr = v[:, N_META:].reshape(B, nb, BLOCK, N_KV_HEADS, HEAD_DIM)
    zpad = jnp.zeros_like(kr[:, :1])
    kb = jnp.concatenate([jnp.concatenate([zpad, kr[:, :-1]], 1), kr], 2)
    vb = jnp.concatenate([jnp.concatenate([zpad, vr[:, :-1]], 1), vr], 2)

    a = jnp.arange(BLOCK)
    kk = jnp.arange(2 * BLOCK)
    blk = jnp.arange(nb)
    dist_band = BLOCK + a[:, None] - kk[None, :]
    mask_band = ((dist_band >= 0) & (dist_band < WINDOW))[None] & \
        ((blk[:, None, None] > 0) | (kk[None, None, :] >= BLOCK))
    q_pos = N_META + blk[:, None] * BLOCK + a[None, :]
    dist_meta = q_pos[:, :, None] - pos_m[None, None, :]

    s_band = jnp.einsum('bnqhgd,bnkhd->bnhgqk', qr, kb).astype(jnp.float32) * scale
    s_band = s_band + head_bias(rel_bias, rel_bucket(dist_band))
    s_band = jnp.where(mask_band[None, :, None, None], s_band, -jnp.inf)
    s_meta = jnp.einsum('bnqhgd,bmhd->bnhgqm', qr, km).astype(jnp.float32) * scale
    s_meta = s_meta + head_bias(rel_bias, rel_bucket(dist_meta))
    p = sink_softmax(jnp.concatenate([s_meta, s_band], -1), sink).astype(v.dtype)
    o_r = jnp.einsum('bnhgqm,bmhd->bnqhgd', p[..., :N_META], vm) + \
        jnp.einsum('bnhgqk,bnkhd->bnqhgd', p[..., N_META:], vb)
    o_r = o_r.reshape(B, S, ATTN_WIDTH)
    return jnp.concatenate([o_m, o_r], 1)

def conformer_conv(u, dw, db, g, b):
    val, gate = jnp.split(u, 2, axis=-1)
    h = val * jax.nn.sigmoid(gate)
    h = lax.conv_general_dilated(h, dw[:, None, :].astype(h.dtype), window_strides=(1,),
                                 padding=[(CONV_WIDTH - 1, 0)],
                                 dimension_numbers=('NWC', 'WIO', 'NWC'),
                                 feature_group_count=CONV_CH_2) + db
    h = layer_norm(h, g, b)
    return jax.nn.silu(h)

def swiglu(t, wg, wu, wd):
    return (jax.nn.silu(t @ wg) * (t @ wu)) @ wd

def moe_swiglu(h, router, wg, wu, wd):
    B, L, D = h.shape
    t = h.reshape(B * L, D)
    logits = (t @ router).astype(jnp.float32)
    vals, idx = lax.top_k(logits, TOP_K)
    gates = jax.nn.softmax(vals, axis=-1)
    combine = jnp.sum(jax.nn.one_hot(idx, N_EXPERTS_2, dtype=jnp.float32) * gates[..., None], 1)
    out = jnp.zeros_like(t)
    for e in range(N_EXPERTS_2):
        out = out + combine[:, e:e + 1].astype(t.dtype) * swiglu(t, wg[e], wu[e], wd[e])
    return out.reshape(B, L, D)

def second_inputs(seed: int = 0) -> dict:
    key = jax.random.key(seed)
    ks = iter(jax.random.split(key, 32))
    n = lambda shape, s: jax.random.normal(next(ks), shape, jnp.float32) * s
    D = D_MODEL
    return {
        "x": n((BATCH, SEQ, D), 1.0),
        "meta_tokens": n((N_META, D), 1.0),
        "emb_ln_g": 1.0 + n((D,), 0.02),
        "emb_ln_b": n((D,), 0.02),
        "rel_bias": n((N_BUCKETS, N_Q_HEADS), 0.5),
        "w_in": n((DEPTH_2, D, IN_WIDTH), D ** -0.5),
        "conv_dw": n((DEPTH_2, CONV_WIDTH, CONV_CH_2), CONV_WIDTH ** -0.5),
        "conv_b": n((DEPTH_2, CONV_CH_2), 0.02),
        "conv_ln_g": 1.0 + n((DEPTH_2, CONV_CH_2), 0.02),
        "conv_ln_b": n((DEPTH_2, CONV_CH_2), 0.02),
        "sinks": n((DEPTH_2, N_Q_HEADS), 0.5),
        "w_attn_proj": n((DEPTH_2, ATTN_WIDTH, D), ATTN_WIDTH ** -0.5),
        "w_conv_proj": n((DEPTH_2, CONV_CH_2, D), CONV_CH_2 ** -0.5),
        "w_out": n((DEPTH_2, D, D), BETA * D ** -0.5),
        "ln1_g": 1.0 + n((DEPTH_2, D), 0.02),
        "ln1_b": n((DEPTH_2, D), 0.02),
        "ffn_w_gate": n((N_DENSE, D, D_FF), D ** -0.5),
        "ffn_w_up": n((N_DENSE, D, D_FF), D ** -0.5),
        "ffn_w_down": n((N_DENSE, D_FF, D), BETA * D_FF ** -0.5),
        "router": n((N_MOE, D, N_EXPERTS_2), D ** -0.5),
        "moe_w_gate": n((N_MOE, N_EXPERTS_2, D, D_EXPERT), D ** -0.5),
        "moe_w_up": n((N_MOE, N_EXPERTS_2, D, D_EXPERT), D ** -0.5),
        "moe_w_down": n((N_MOE, N_EXPERTS_2, D_EXPERT, D), BETA * D_EXPERT ** -0.5),
        "ln2_g": 1.0 + n((DEPTH_2, D), 0.02),
        "ln2_b": n((DEPTH_2, D), 0.02),
    }

def second_block(x, meta_tokens, emb_ln_g, emb_ln_b, rel_bias, w_in, conv_dw, conv_b,
              conv_ln_g, conv_ln_b, sinks, w_attn_proj, w_conv_proj, w_out, ln1_g, ln1_b,
              ffn_w_gate, ffn_w_up, ffn_w_down, router, moe_w_gate, moe_w_up, moe_w_down,
              ln2_g, ln2_b):
    B = x.shape[0]
    meta = jnp.broadcast_to(meta_tokens[None].astype(x.dtype), (B, N_META, D_MODEL))
    h = layer_norm(jnp.concatenate([meta, x], axis=1), emb_ln_g, emb_ln_b)
    L = h.shape[1]
    for i in range(DEPTH_2):
        u = h @ w_in[i]
        q = u[..., :Q_END].reshape(B, L, N_Q_HEADS, HEAD_DIM)
        k = u[..., Q_END:K_END].reshape(B, L, N_KV_HEADS, HEAD_DIM)
        v = u[..., K_END:V_END].reshape(B, L, N_KV_HEADS, HEAD_DIM)
        y_attn = sliding_window_attention(q, k, v, sinks[i], rel_bias) @ w_attn_proj[i]
        y_conv = conformer_conv(u[..., V_END:GLU_END], conv_dw[i], conv_b[i],
                                conv_ln_g[i], conv_ln_b[i]) @ w_conv_proj[i]
        mix = (jax.nn.sigmoid(u[..., GLU_END:GA_END]) * y_attn
               + jax.nn.sigmoid(u[..., GA_END:GC_END]) * y_conv) @ w_out[i]
        h = layer_norm(ALPHA * h + mix, ln1_g[i], ln1_b[i])
        j = i // 2
        if i % 2 == 0:
            f = swiglu(h, ffn_w_gate[j], ffn_w_up[j], ffn_w_down[j])
        else:
            f = moe_swiglu(h, router[j], moe_w_gate[j], moe_w_up[j], moe_w_down[j])
        h = layer_norm(ALPHA * h + f, ln2_g[i], ln2_b[i])
    return h[:, N_META:]


def setup_inputs(seed=0):
    out = dict(first_inputs(seed))
    for name, value in second_inputs(seed + 1).items():
        if name != "x":
            out[name + "_2"] = value
    return out


def reference(
    x, norm1_w, w_in, conv_w, conv_b, gdn_A_log, gdn_dt_bias, gdn_norm_w, ssd_A_log,
    ssd_dt_bias, ssd_D, ssd_norm_w, w_out, norm2_w, w_router, w_gate, w_up, w_down,
    final_norm_w, meta_tokens_2, emb_ln_g_2, emb_ln_b_2, rel_bias_2, w_in_2, conv_dw_2,
    conv_b_2, conv_ln_g_2, conv_ln_b_2, sinks_2, w_attn_proj_2, w_conv_proj_2, w_out_2, ln1_g_2,
    ln1_b_2, ffn_w_gate_2, ffn_w_up_2, ffn_w_down_2, router_2, moe_w_gate_2, moe_w_up_2,
    moe_w_down_2, ln2_g_2, ln2_b_2,
):
    x = first_block(
        x, norm1_w, w_in, conv_w, conv_b, gdn_A_log, gdn_dt_bias, gdn_norm_w, ssd_A_log,
        ssd_dt_bias, ssd_D, ssd_norm_w, w_out, norm2_w, w_router, w_gate, w_up, w_down,
        final_norm_w,
    )
    return second_block(
        x, meta_tokens_2, emb_ln_g_2, emb_ln_b_2, rel_bias_2, w_in_2, conv_dw_2, conv_b_2,
        conv_ln_g_2, conv_ln_b_2, sinks_2, w_attn_proj_2, w_conv_proj_2, w_out_2, ln1_g_2,
        ln1_b_2, ffn_w_gate_2, ffn_w_up_2, ffn_w_down_2, router_2, moe_w_gate_2, moe_w_up_2,
        moe_w_down_2, ln2_g_2, ln2_b_2,
    )


_drawn_inputs = setup_inputs


def setup_inputs(seed=0):
    import zlib

    import numpy as np

    out = dict(_drawn_inputs(seed))
    spreads = {}
    factors = {'conv_b': 3.436,
     'gdn_norm_w': 4.659,
     'ssd_D': 6.439,
     'ssd_norm_w': 3.305,
     'norm2_w': 3.162,
     'conv_b_2': 7.308,
     'conv_ln_g_2': 8.0,
     'conv_ln_b_2': 8.0,
     'sinks_2': 21.462,
     'rel_bias_2': 3.278}
    for name, (base, spread) in spreads.items():
        noise = np.random.default_rng([zlib.crc32(name.encode()), seed]).standard_normal(out[name].shape)
        drawn = base * np.exp(spread * noise) if base else spread * noise
        out[name] = __import__('jax').numpy.asarray(drawn.astype(out[name].dtype))
    for name, factor in factors.items():
        out[name] = (out[name] * factor).astype(out[name].dtype)
    return out
```

```python
from contextlib import ExitStack

import numpy as np

import concourse.bass as bass
from concourse import mybir

F32 = mybir.dt.float32
ACT = mybir.ActivationFunctionType
ALU = mybir.AluOpType
AX = mybir.AxisListType

P = 128
BANK = 512
SEQ, D = 512, 1024
TILES = SEQ // P
DK = D // P
EPS = 1e-6

GH, SH, SG, SHD = 8, 16, 2, 64
CONV_CH = 4608
CCH = CONV_CH // P
Q0, K0, V0, X0, B0, C0 = 0, 8, 16, 24, 32, 34
TAPS, PAD = 7, 3
GATE_CH = 2048
SCAL0 = CONV_CH + GATE_CH
SCAL = 64
NG = 48
LEVELS = 7
(F_G, F_GC, F_BETA, F_NBETA, F_EGC, F_W, F_EGL, F_DT, F_DTW) = range(9)
PLANES = 9

COL_NORM1, COL_NORM2, COL_SSD, COL_GDN, COL_EPS = 0, 8, 16, 24, 25
NCOL1 = 27

ID0, TRI0, ONE0, NCONST = 0, P, 3 * P, 4 * P


def shape_constants():
    r = np.arange(P)
    parts = [np.eye(P), r[:, None] <= r[None, :], r[:, None] >= r[None, :], np.ones((P, P))]
    return np.concatenate([np.asarray(p, np.float32) for p in parts], axis=1)


def level_constants():
    r = np.arange(P)
    parts = []
    for lev in range(LEVELS):
        b = r >> lev
        low = (b[:, None] % 2 == 1) & (b[None, :] == b[:, None] - 1)
        parts += [low, low.T]
    return np.concatenate([np.asarray(p, np.float32) for p in parts], axis=1)


class Core:

    def __init__(self, nc, ctx):
        self.nc, self.ctx, self.n = nc, ctx, 0
        self.sems, self.sem_ctx = [], ExitStack()

    def sem(self, name):
        self.n += 1
        self.sems.append(self.sem_ctx.enter_context(self.nc.semaphore(f"{name}_{self.n}")))
        return self.sems[-1]

    def recycle_semaphores(self):
        with self.block() as block:

            @block.gpsimd
            def _(pool):
                for s in self.sems:
                    pool.sem_clear(s)

        self.sem_ctx.close()
        self.sems, self.sem_ctx = [], ExitStack()

    def sb(self, ctx, name, shape):
        self.n += 1
        return ctx.enter_context(self.nc.sbuf_tensor(f"{name}_{self.n}", shape, F32))

    def ps(self, ctx, name, shape):
        self.n += 1
        return ctx.enter_context(self.nc.psum_tensor(f"{name}_{self.n}", shape, F32))

    def block(self):
        return self.nc.Block(no_gpsimd_drain=True)


class Steps:

    def __init__(self, eng, sem, base=0):
        self.eng, self.sem, self.base, self.n = eng, sem, base, 0

    def mark(self, instruction):
        instruction.then_inc(self.sem, 1)
        self.n += 1

    def wait(self):
        self.eng.wait_ge(self.sem, self.base + self.n)


def over(ap, n):
    p, a = ap.shape
    return ap.unsqueeze(2).to_broadcast([p, a, n])


def each(ap, n):
    p, a = ap.shape
    return ap.unsqueeze(1).to_broadcast([p, n, a])


def tiles(ap, n=TILES):
    return ap.rearrange("p (t c) -> p t c", t=n)


def load_constants(core, A):
    nc = core.nc
    landed = core.sem("constants_landed")
    with core.block() as block:

        @block.sync
        def _(sp):
            sp.dma_start(core.cst[:, :], A["shapes"]).then_inc(landed, 16)
            sp.dma_start(core.cols[:, :], A["columns"]).then_inc(landed, 16)
            sp.dma_start(core.hid[:, 0:TILES, :], A["x"][0].rearrange("(t p) d -> p t d", p=P)).then_inc(landed, 16)
            sp.wait_ge(landed, 48)


def rms_to_features(core, gain, feat, tok=None):
    with ExitStack() as ctx:
        scaled_rows = tok if tok is not None else core.sb(ctx, "scaled_rows", [P, TILES, D])
        squares = core.sb(ctx, "squares", [P, D])
        stat = core.sb(ctx, "stat", [P, 4, TILES])
        turned = core.ps(ctx, "turned", [P, DK, BANK])
        squared, stats, root, scaled, transposed = (
            core.sem(s) for s in ("squared", "stats", "root", "scaled", "transposed"))
        ident = core.cst[:, ID0:ID0 + P]
        with core.block() as block:

            @block.scalar
            def _(act):
                for t in range(TILES):
                    if t:
                        act.wait_ge(squared, t)
                    act.activation(squares[:, :], core.hid[:, t, :], ACT.Square,
                                   accum_out=stat[:, 0, t:t + 1]).then_inc(squared, 1)
                act.wait_ge(stats, 1)
                act.activation(stat[:, 2, :], stat[:, 1, :], ACT.Sqrt).then_inc(root, 1)
                for k in range(0, DK, 2):
                    act.wait_ge(transposed, k + 1)
                    act.activation(feat[:, k, :], turned[:, k, :], ACT.Copy, scale=gain[:, k:k + 1])

            @block.vector
            def _(dve):
                dve.wait_ge(squared, TILES)
                dve.tensor_scalar(stat[:, 1, :], stat[:, 0, :], 1.0 / D, EPS, ALU.mult, ALU.add).then_inc(stats, 1)
                dve.wait_ge(root, 1)
                dve.reciprocal(stat[:, 3, :], stat[:, 2, :]).then_inc(stats, 1)
                dve.wait_ge(stats, 2)
                for t in range(TILES):
                    dve.tensor_scalar(scaled_rows[:, t, :], core.hid[:, t, :], stat[:, 3, t:t + 1], None,
                                      ALU.mult).then_inc(scaled, 1)
                for k in range(1, DK, 2):
                    dve.wait_ge(transposed, k + 1)
                    dve.tensor_scalar(feat[:, k, :], turned[:, k, :], gain[:, k:k + 1], None, ALU.mult)

            @block.tensor
            def _(pe):
                for k in range(DK):
                    for t in range(TILES):
                        if k == 0:
                            pe.wait_ge(scaled, t + 1)
                        last = pe.transpose(turned[:, k, t * P:(t + 1) * P],
                                            scaled_rows[:, t, k * P:(k + 1) * P], ident)
                    last.then_inc(transposed, 1)


def conv_projection(core, A):
    w_in = A["w_in"][0].rearrange("(k p) n -> p k n", p=P)
    GRP = BANK // P
    groups = CCH // GRP
    with ExitStack() as ctx:
        w = core.sb(ctx, "w", [P, 2, DK, BANK])
        taps = core.sb(ctx, "taps", [P, CCH, TAPS + 1])
        padded = core.sb(ctx, "padded", [P, 2, SEQ + 2 * PAD])
        mixed = core.sb(ctx, "mixed", [P, 2, SEQ])
        proj = core.ps(ctx, "proj", [P, 2, BANK])
        taps_in = core.sem("taps_in")
        w_in_sem = [core.sem("w_landed") for _ in range(2)]
        w_used, projected, filled, tapped, convolved, activated, zeroed = (
            core.sem(s) for s in ("w_used", "projected", "filled", "tapped", "convolved", "activated", "zeroed"))

        def turns(eng, body):
            with eng.Fori(0, groups // 2) as i:
                for b in range(2):
                    body(i, b, i * 2 + b)
            body(groups // 2, 0, groups - 1)

        with core.block() as block:

            @block.sync
            def _(sp):
                sp.dma_start(taps[:, :, :], A["conv_cols"]).then_inc(taps_in, 16)

                def load(i, b, g):
                    sp.wait_ge(w_used, g + 1)
                    sp.dma_start(w[:, b, :, :], w_in[:, :, bass.ds(g * BANK, BANK)]).then_inc(w_in_sem[b], 16)

                turns(sp, load)

            @block.gpsimd
            def _(pool):
                pool.memset(padded[:, :, :], 0.0).then_inc(zeroed, 1)

            @block.tensor
            def _(pe):
                pe.sem_inc(w_used, 2)

                def multiply(i, b, g):
                    pe.wait_ge(w_in_sem[b], i * 16 + 16)
                    for c in range(GRP):
                        pe.wait_ge(filled, g * GRP + c + 1)
                        for k in range(DK):
                            last = pe.matmul(proj[:, c % 2, :], w[:, b, k, c * P:(c + 1) * P],
                                             core.feat[:, k, :], start=k == 0, stop=k == DK - 1)
                        last.then_inc(projected, 1)
                    pe.wait_ge(projected, g * GRP + GRP)
                    pe.sem_inc(w_used, 1)

                turns(pe, multiply)

            @block.scalar
            def _(act):
                act.sem_inc(filled, 2)
                act.sem_inc(activated, 2)
                act.wait_ge(zeroed, 1)

                def chunks(i, b, g):
                    for c in range(GRP):
                        n = g * GRP + c
                        act.wait_ge(projected, n + 1)
                        act.wait_ge(convolved, n + 1)
                        act.activation(padded[:, c % 2, PAD:PAD + SEQ], proj[:, c % 2, :], ACT.Copy).then_inc(filled, 1)
                        act.wait_ge(convolved, n + 3)
                        act.activation(core.chan[:, bass.ds(n, 1), :].rearrange("p a t -> p (a t)"),
                                       mixed[:, c % 2, :], ACT.Silu).then_inc(activated, 1)

                turns(act, chunks)

            @block.vector
            def _(dve):
                dve.sem_inc(convolved, 2)
                dve.wait_ge(taps_in, 16)

                def chunks(i, b, g):
                    for c in range(GRP):
                        n = g * GRP + c
                        out, src = mixed[:, c % 2, :], padded[:, c % 2, :]

                        def tap(j):
                            return taps[:, bass.ds(n, 1), j]

                        dve.wait_ge(filled, n + 3)
                        dve.wait_ge(activated, n + 1)
                        dve.tensor_scalar(out, src[:, 0:SEQ], tap(0), tap(TAPS), ALU.mult, ALU.add).then_inc(tapped, 1)
                        for j in range(1, TAPS):
                            dve.wait_ge(tapped, n * (TAPS - 1) + j)
                            dve.scalar_tensor_tensor(out=out, in0=src[:, j:j + SEQ], scalar=tap(j), in1=out,
                                                     op0=ALU.mult, op1=ALU.add
                                                     ).then_inc(convolved if j == TAPS - 1 else tapped, 1)

                turns(dve, chunks)


def channels_to_tokens(core):
    with ExitStack() as ctx:
        turned = core.ps(ctx, "turned", [P, 4, BANK])
        transposed, moved_a, moved_v = (core.sem(s) for s in ("transposed", "moved_a", "moved_v"))
        stage_in = core.sb(ctx, "stage_in", [P, 2, SEQ])
        ident = core.cst[:, ID0:ID0 + P]
        with core.block() as block:

            picked = core.sem("picked")

            @block.gpsimd
            def _(pool):
                def pick(n, src):
                    pool.wait_ge(transposed, n * 2 + 1)
                    pool.tensor_copy(stage_in[:, :, :], src).then_inc(picked, 1)

                with pool.Fori(0, 8) as i:
                    pick(i, core.chan[:, bass.ds(i * 2 + V0, 2), :])
                pick(8, core.chan[:, B0:B0 + 2, :])

            @block.tensor
            def _(pe):
                pe.sem_inc(transposed, 1)
                pe.sem_inc(moved_a, 1)
                pe.sem_inc(moved_v, 1)
                with pe.Fori(0, 9) as i:
                    pe.wait_ge(picked, i + 1)
                    pe.wait_ge(moved_a, i + 1)
                    pe.wait_ge(moved_v, i + 1)
                    for e in range(2):
                        for t in range(TILES):
                            last = pe.transpose(turned[:, e, t * P:(t + 1) * P], stage_in[:, e, t * P:(t + 1) * P], ident)
                        last.then_inc(transposed, 1)

            def move(eng, copy, moved, e):
                with eng.Fori(0, 4) as i:
                    eng.wait_ge(transposed, i * 2 + 2 + e)
                    copy(core.tok_v[:, :, bass.ds((i * 2 + e) * P, P)], tiles(turned[:, e, :])).then_inc(moved, 1)
                with eng.Fori(0, 4) as i:
                    eng.wait_ge(transposed, i * 2 + 10 + e)
                    copy(core.tok_x[:, :, bass.ds((i * 2 + e) * P, P)], tiles(turned[:, e, :])).then_inc(moved, 1)
                eng.wait_ge(transposed, 18 + e)
                copy(core.tok_b[:, :, e * P:(e + 1) * P], tiles(turned[:, e, :])).then_inc(moved, 1)

            @block.scalar
            def _(act):
                move(act, lambda o, i: act.activation(o, i, ACT.Copy), moved_a, 0)

            @block.vector
            def _(dve):
                move(dve, lambda o, i: dve.tensor_copy(o, i), moved_v, 1)


def token_scalars(core, A):
    sc = core.scal
    with ExitStack() as ctx:
        w = core.sb(ctx, "w", [P, DK, SCAL])
        rows = core.sb(ctx, "rows", [P, 2, NG])
        raw = core.sb(ctx, "raw", [P, TILES, SCAL])
        a = core.sb(ctx, "a", [P, TILES, NG])
        b = core.sb(ctx, "b", [P, TILES, NG])
        neg_a = core.sb(ctx, "neg_a", [P, NG])
        proj = core.ps(ctx, "proj", [P, TILES, SCAL])
        sums = core.ps(ctx, "sums", [P, 2, BANK])
        whole = core.ps(ctx, "whole", [P, BANK])
        landed, projected, s_act, s_dve, summed = (
            core.sem(s) for s in ("landed", "projected", "s_act", "s_dve", "summed"))
        nb = 2 * GH
        n = TILES * NG
        flat = lambda ap: ap.rearrange("p t n -> p (t n)")

        with core.block() as block:

            @block.sync
            def _(sp):
                sp.dma_start(w[:, :, :], A["w_in"][0].rearrange("(k p) n -> p k n", p=P)[:, :, SCAL0:]).then_inc(landed, 16)
                sp.dma_start(rows[:, :, :].rearrange("p a n -> p (a n)"),
                             A["scal_rows"].to_broadcast([P, 2 * NG])).then_inc(landed, 16)

            @block.tensor
            def _(pe):
                pe.wait_ge(landed, 32)
                for t in range(TILES):
                    for k in range(DK):
                        last = pe.matmul(proj[:, t, :], core.feat[:, k, t * P:(t + 1) * P], w[:, k, :],
                                         start=k == 0, stop=k == DK - 1)
                last.then_inc(projected, 1)
                pe.wait_ge(s_dve, 9)
                for d in range(2):
                    for t in range(TILES):
                        last = pe.matmul(sums[:, d, t * NG:(t + 1) * NG], core.cst[:, TRI0 + d * P:TRI0 + (d + 1) * P],
                                         sc[:, F_G, t, :], start=True, stop=True)
                last.then_inc(summed, 1)
                pe.matmul(whole[:, 0:n], core.cst[:, ONE0:ONE0 + P], flat(sc[:, F_G, :, :]),
                          start=True, stop=True).then_inc(summed, 1)

            @block.scalar
            def _(act):
                act.wait_ge(landed, 32)
                act.activation(neg_a[:, :], rows[:, 1, :], ACT.Exp).then_inc(s_act, 1)
                act.wait_ge(s_dve, 4)
                act.activation(flat(b[:, :, :]), flat(b[:, :, :]), ACT.Exp).then_inc(s_act, 1)
                act.wait_ge(s_act, 2)
                act.activation(flat(b[:, :, :]), flat(b[:, :, :]), ACT.Ln, bias=1.0).then_inc(s_act, 1)
                act.activation(sc[:, F_BETA, :, 0:nb], raw[:, :, 0:nb], ACT.Exp, scale=-1.0).then_inc(s_act, 1)
                act.wait_ge(s_dve, 14)
                act.activation(flat(sc[:, F_EGC, :, :]), flat(sc[:, F_GC, :, :]), ACT.Exp).then_inc(s_act, 1)
                act.activation(flat(sc[:, F_W, :, :]), flat(sc[:, F_W, :, :]), ACT.Exp).then_inc(s_act, 1)
                act.activation(flat(sc[:, F_EGL, :, :]), whole[:, 0:n], ACT.Exp).then_inc(s_act, 1)

            @block.vector
            def _(dve):
                steps = Steps(dve, s_dve)
                dve.wait_ge(projected, 1)
                steps.mark(dve.tensor_copy(raw[:, :, :], proj[:, :, :]))
                steps.wait()
                steps.mark(dve.tensor_tensor(a[:, :, :], raw[:, :, nb:], each(rows[:, 0, :], TILES), ALU.add))
                steps.wait()
                steps.mark(dve.tensor_scalar(flat(b[:, :, :]), flat(a[:, :, :]), -1.0, None, ALU.mult))
                steps.wait()
                steps.mark(dve.tensor_tensor(b[:, :, :], a[:, :, :], b[:, :, :], ALU.min))
                dve.wait_ge(s_act, 3)
                steps.wait()
                steps.mark(dve.scalar_tensor_tensor(out=flat(sc[:, F_DT, :, :]), in0=flat(a[:, :, :]), scalar=0.0,
                                                    in1=flat(b[:, :, :]), op0=ALU.max, op1=ALU.add))
                dve.wait_ge(s_act, 4)
                steps.mark(dve.tensor_scalar(sc[:, F_BETA, :, 0:nb], sc[:, F_BETA, :, 0:nb], 1.0, None, ALU.add))
                steps.wait()
                steps.mark(dve.reciprocal(sc[:, F_BETA, :, 0:nb], sc[:, F_BETA, :, 0:nb]))
                steps.wait()
                steps.mark(dve.tensor_scalar(sc[:, F_NBETA, :, 0:nb], sc[:, F_BETA, :, 0:nb], -1.0, None, ALU.mult))
                steps.mark(dve.scalar_tensor_tensor(out=sc[:, F_G, :, :], in0=sc[:, F_DT, :, :], scalar=-1.0,
                                                    in1=each(neg_a[:, :], TILES), op0=ALU.mult, op1=ALU.mult))
                dve.wait_ge(summed, 2)
                for d in range(2):
                    for lo, hi in ((d * GH, (d + 1) * GH), (2 * GH + d * SH, 2 * GH + (d + 1) * SH)):
                        s = sums[:, d, 0:n].rearrange("p (t n) -> p t n", n=NG)[:, :, lo:hi]
                        steps.mark(dve.tensor_copy(sc[:, F_GC, :, lo:hi], s))
                steps.wait()
                steps.mark(dve.tensor_tensor(flat(sc[:, F_W, :, :]), whole[:, 0:n], flat(sc[:, F_GC, :, :]), ALU.subtract))
                dve.wait_ge(s_act, 6)
                dve.tensor_tensor(flat(sc[:, F_DTW, :, :]), flat(sc[:, F_DT, :, :]), flat(sc[:, F_W, :, :]), ALU.mult)


def normalize_qk(core):
    with ExitStack() as ctx:
        sq = core.sb(ctx, "sq", [P, 2, SEQ])
        root = core.sb(ctx, "root", [P, 2, SEQ])
        inv = core.sb(ctx, "inv", [P, 2, SEQ])
        total = core.ps(ctx, "total", [P, 2, BANK])
        squared, summed, rooted, scaled, inverted = (
            core.sem(s) for s in ("squared", "summed", "rooted", "scaled", "inverted"))
        with core.block() as block:

            def chunk(e, i):
                return core.chan[:, bass.ds(i + e * K0, 1), :].rearrange("p a t -> p (a t)")

            @block.scalar
            def _(act):
                act.sem_inc(rooted, 2)
                with act.Fori(0, GH) as i:
                    for e in range(2):
                        act.wait_ge(summed, i * 2 + e + 1)
                        act.activation(sq[:, e, :], chunk(e, i), ACT.Square).then_inc(squared, 1)
                    for e, s in ((0, float(P)), (1, 1.0)):
                        act.wait_ge(summed, i * 2 + e + 3)
                        act.wait_ge(scaled, i * 2 + e + 1)
                        act.activation(root[:, e, :], total[:, e, :], ACT.Sqrt, scale=s,
                                       bias=core.cols[:, COL_EPS + e:COL_EPS + e + 1]).then_inc(rooted, 1)

            @block.tensor
            def _(pe):
                pe.sem_inc(summed, 2)
                with pe.Fori(0, GH) as i:
                    for e in range(2):
                        pe.wait_ge(squared, i * 2 + e + 1)
                        pe.wait_ge(rooted, i * 2 + e + 1)
                        pe.matmul(total[:, e, :], core.cst[:, ONE0:ONE0 + P], sq[:, e, :],
                                  start=True, stop=True).then_inc(summed, 1)

            @block.vector
            def _(dve):
                dve.sem_inc(scaled, 2)
                with dve.Fori(0, GH) as i:
                    for e in range(2):
                        dve.wait_ge(rooted, i * 2 + e + 3)
                        dve.reciprocal(inv[:, e, :], root[:, e, :]).then_inc(inverted, 1)
                        dve.wait_ge(inverted, i * 2 + e + 1)
                        dve.tensor_tensor(chunk(e, i), chunk(e, i), inv[:, e, :], ALU.mult).then_inc(scaled, 1)


def gated_delta(core, A):
    FIELDS = 7
    with ExitStack() as ctx:
        sb = lambda name, *shape: core.sb(ctx, name, [P, *shape])
        qh, kh, ktok, vh = (sb(s, SEQ) for s in ("qh", "kh", "ktok", "vh"))
        hs = sb("hs", FIELDS * TILES, 2)
        levels = sb("levels", LEVELS * 2 * P)
        levels_in = core.sem("levels_in")
        dec, am, qm, tm, um, xm = (sb(s, 2, SEQ) for s in ("dec", "am", "qm", "tm", "um", "xm"))
        st, rest, uu, uw = (sb(s, 2, P) for s in ("st", "rest", "uu", "uw"))
        px, py, pu = (core.ps(ctx, s, [P, 2, BANK]) for s in ("px", "py", "pu"))
        names = ("head_done copied picked products ktok_out clamped decayed masked x_made x_masked y_made "
                 "t_updated states_in rest_made v_made u_made kept o_made")
        (head_done, copied, picked, products, ktok_out, clamped, decayed, masked, x_made, x_masked, y_made,
         t_updated, states_in, rest_made, v_made, u_made, kept, o_made) = (core.sem(s) for s in names.split())
        ident = core.cst[:, ID0:ID0 + P]

        def tl(t):
            return slice(t * P, (t + 1) * P)

        def field(f, t, d):
            return hs[:, f * TILES + t, d:d + 1]

        def tri(d):
            return core.cst[:, TRI0 + d * P:TRI0 + (d + 1) * P]

        with core.block() as block:

            @block.sync
            def _(sp):
                sp.dma_start(levels[:, :], A["level_shapes"]).then_inc(levels_in, 16)

            @block.scalar
            def _(act):
                with act.Fori(0, GH) as h:
                    act.wait_ge(head_done, h + 1)
                    for buf, base in ((qh, Q0), (kh, K0)):
                        act.activation(buf[:, :], core.chan[:, bass.ds(h + base, 1), :].rearrange("p a t -> p (a t)"),
                                       ACT.Copy).then_inc(copied, 1)
                    act.wait_ge(products, h * 5 + 1)
                    act.activation(ktok[:, :], pu[:, 0, :], ACT.Copy).then_inc(ktok_out, 1)
                    for d in range(2):
                        act.wait_ge(clamped, h * 2 + d + 1)
                        act.activation(dec[:, d, :], dec[:, d, :], ACT.Exp).then_inc(decayed, 1)

            @block.gpsimd
            def _(pool):
                with pool.Fori(0, GH) as h:
                    pool.wait_ge(head_done, h + 1)
                    src = core.scal[:, 0:FIELDS, :, 0:2 * GH].rearrange("p f t (d h) -> p (f t) d h", d=2)
                    pool.tensor_copy(hs[:, :, :], src[:, :, :, bass.ds(h, 1)].rearrange("p a d o -> p a (d o)")).then_inc(picked, 1)
                    pool.tensor_copy(tiles(vh[:, :]), core.tok_v[:, :, bass.ds(h * P, P)]).then_inc(picked, 1)
                    for d in range(2):
                        pool.tensor_copy(tiles(tm[:, d, :]), each(ident, TILES)).then_inc(picked, 1)
                        pool.tensor_copy(tiles(um[:, d, :]), each(ident, TILES)).then_inc(picked, 1)
                    pool.memset(st[:, :, :], 0.0).then_inc(picked, 1)

            @block.tensor
            def _(pe):
                with pe.Fori(0, GH) as h:
                    pe.wait_ge(copied, h * 2 + 2)
                    pe.wait_ge(head_done, h + 1)
                    for t in range(TILES):
                        last = pe.transpose(pu[:, 0, tl(t)], kh[:, tl(t)], ident)
                    last.then_inc(products, 1)
                    for t in range(TILES):
                        last = pe.matmul(py[:, 0, tl(t)], kh[:, tl(t)], kh[:, tl(t)], start=True, stop=True)
                    last.then_inc(products, 1)
                    for t in range(TILES):
                        last = pe.matmul(py[:, 1, tl(t)], kh[:, tl(t)], qh[:, tl(t)], start=True, stop=True)
                    last.then_inc(products, 1)
                    pe.wait_ge(picked, h * 7 + 7)
                    for d in range(2):
                        for t in range(TILES):
                            last = pe.matmul(px[:, d, tl(t)], field(F_G, t, d).to_broadcast([P, P]), tri(d),
                                             start=True, stop=True)
                        last.then_inc(products, 1)
                    with pe.Fori(0, LEVELS) as lev:
                        n = h * LEVELS + lev
                        pe.wait_ge(ktok_out, h + 1)
                        pe.wait_ge(masked, h * 2 + 2)
                        for d in range(2):
                            pe.wait_ge(t_updated, n * 2 + d + 1)
                            for t in range(TILES):
                                last = pe.matmul(px[:, d, tl(t)], am[:, d, tl(t)], tm[:, d, tl(t)], start=True, stop=True)
                            last.then_inc(x_made, 1)
                        for d in range(2):
                            pe.wait_ge(x_masked, n * 2 + d + 1)
                            for t in range(TILES):
                                pe.matmul(py[:, d, tl(t)], um[:, d, tl(t)], xm[:, d, tl(t)], start=True, stop=True)
                            for t in range(TILES):
                                last = pe.matmul(pu[:, d, tl(t)], xm[:, d, tl(t)], um[:, d, tl(t)], start=True, stop=True)
                            last.then_inc(y_made, 1)
                    for d in range(2):
                        pe.wait_ge(t_updated, (h * LEVELS + LEVELS) * 2 + d + 1)
                    for s in range(TILES):
                        for d in range(2):
                            n = h * 2 * TILES + 2 * s + d
                            t = s if d == 0 else TILES - 1 - s
                            pe.wait_ge(kept, n + 1)
                            pe.matmul(px[:, d, tl(0)], kh[:, tl(t)], st[:, d, :], start=True, stop=True)
                            pe.matmul(px[:, d, tl(1)], qh[:, tl(t)], st[:, d, :], start=True, stop=True).then_inc(states_in, 1)
                        for d in range(2):
                            n = h * 2 * TILES + 2 * s + d
                            t = s if d == 0 else TILES - 1 - s
                            pe.wait_ge(rest_made, n + 1)
                            pe.matmul(py[:, d, tl(0)], um[:, d, tl(t)], rest[:, d, :], start=True, stop=True).then_inc(v_made, 1)
                        for d in range(2):
                            n = h * 2 * TILES + 2 * s + d
                            t = s if d == 0 else TILES - 1 - s
                            pe.wait_ge(u_made, n + 1)
                            pe.matmul(pu[:, d, tl(0)], ktok[:, tl(t)], uw[:, d, :], start=True, stop=True)
                            pe.matmul(pu[:, d, tl(1)], qm[:, d, tl(t)], uu[:, d, :], start=True, stop=True).then_inc(o_made, 1)

            @block.vector
            def _(dve):
                dve.sem_inc(head_done, 1)
                dve.sem_inc(t_updated, 2)
                dve.wait_ge(levels_in, 16)
                dve.sem_inc(kept, 2)
                own = core.sem("own")
                PER = 4 + 2 * 2 * TILES
                with dve.Fori(0, GH) as h:
                    steps = Steps(dve, own, h * PER)
                    dve.wait_ge(picked, h * 7 + 7)
                    for d in range(2):
                        dve.wait_ge(products, h * 5 + 4 + d)
                        for t in range(TILES):
                            last = dve.tensor_scalar(dec[:, d, tl(t)], px[:, d, tl(t)], field(F_GC, t, d), 0.0,
                                                     ALU.subtract, ALU.min)
                        last.then_inc(clamped, 1)
                    for d in range(2):
                        dve.wait_ge(decayed, h * 2 + d + 1)
                        steps.mark(dve.tensor_tensor(tiles(dec[:, d, :]), tiles(dec[:, d, :]), each(tri(d), TILES), ALU.mult))
                        steps.wait()
                        for t in range(TILES):
                            last = dve.scalar_tensor_tensor(out=am[:, d, tl(t)], in0=py[:, 0, tl(t)], scalar=field(F_BETA, t, d),
                                                            in1=dec[:, d, tl(t)], op0=ALU.mult, op1=ALU.mult)
                        steps.mark(last)
                        dve.tensor_tensor(qm[:, d, :], py[:, 1, :], dec[:, d, :], ALU.mult).then_inc(masked, 1)
                    with dve.Fori(0, LEVELS) as lev:
                        n = h * LEVELS + lev
                        for d in range(2):
                            dve.wait_ge(x_made, n * 2 + d + 1)
                            mask = levels[:, bass.ds(lev * (2 * P) + d * P, P)]
                            dve.tensor_tensor(tiles(xm[:, d, :]), tiles(px[:, d, :]), each(mask, TILES), ALU.mult).then_inc(x_masked, 1)
                        for d in range(2):
                            dve.wait_ge(y_made, n * 2 + d + 1)
                            dve.tensor_tensor(tm[:, d, :], tm[:, d, :], py[:, d, :], ALU.subtract)
                            dve.tensor_tensor(um[:, d, :], um[:, d, :], pu[:, d, :], ALU.subtract).then_inc(t_updated, 1)
                    for s in range(TILES):
                        for d in range(2):
                            n = h * 2 * TILES + 2 * s + d
                            t = s if d == 0 else TILES - 1 - s
                            out = core.o_acc[:, t, bass.ds(h * P, P)]
                            dve.wait_ge(states_in, n + 1)
                            dve.scalar_tensor_tensor(out=rest[:, d, :], in0=px[:, d, tl(0)], scalar=field(F_EGC, t, d),
                                                     in1=vh[:, tl(t)], op0=ALU.mult, op1=ALU.subtract).then_inc(rest_made, 1)
                            if s < TILES // 2:
                                steps.mark(dve.tensor_scalar(out, px[:, d, tl(1)], field(F_EGC, t, d), None, ALU.mult))
                            else:
                                steps.wait()
                                steps.mark(dve.scalar_tensor_tensor(out=out, in0=px[:, d, tl(1)], scalar=field(F_EGC, t, d),
                                                                    in1=out, op0=ALU.mult, op1=ALU.add))
                        for d in range(2):
                            n = h * 2 * TILES + 2 * s + d
                            t = s if d == 0 else TILES - 1 - s
                            dve.wait_ge(v_made, n + 1)
                            dve.tensor_scalar(uu[:, d, :], py[:, d, tl(0)], field(F_NBETA, t, d), None, ALU.mult)
                            dve.tensor_scalar(uw[:, d, :], py[:, d, tl(0)], field(F_NBETA, t, d), field(F_W, t, d),
                                              ALU.mult, ALU.mult).then_inc(u_made, 1)
                        for d in range(2):
                            n = h * 2 * TILES + 2 * s + d
                            t = s if d == 0 else TILES - 1 - s
                            out = core.o_acc[:, t, bass.ds(h * P, P)]
                            dve.wait_ge(o_made, n + 1)
                            steps.wait()
                            steps.mark(dve.tensor_tensor(out, out, pu[:, d, tl(1)], ALU.add))
                            dve.scalar_tensor_tensor(out=st[:, d, :], in0=st[:, d, :], scalar=field(F_EGL, t, d),
                                                     in1=pu[:, d, tl(0)], op0=ALU.mult, op1=ALU.add).then_inc(kept, 1)
                    steps.wait()
                    dve.wait_ge(kept, h * 2 * TILES + 2 * TILES + 2)
                    dve.sem_inc(head_done, 1)
                    assert steps.n == PER


def ssd(core):
    HG = SH // SG
    with ExitStack() as ctx:
        sb = lambda name, *shape: core.sb(ctx, name, [P, *shape])
        cbt = sb("cbt", 4, P)
        cback = sb("cback", 2, P)
        btok = sb("btok", 2, SG * P)
        gs = sb("gs", 2 * SH)
        cb = sb("cb", SG, P)
        dec = sb("dec", 2, 2, SEQ)
        state = sb("state", 2, SG, BANK)
        xw = sb("xw", 2, SG, BANK)
        part = sb("part", BANK)
        pc = core.ps(ctx, "pc", [P, BANK])
        pr = core.ps(ctx, "pr", [P, 2, BANK])
        pyy = core.ps(ctx, "pyy", [P, 2, BANK])
        pi = core.ps(ctx, "pi", [P, BANK])
        pst = core.ps(ctx, "pst", [P, BANK])
        (turn_done, copied, picked, cb_made, cb_out, r_made, clamped, decayed, weighed, y_made, i_made, i_read,
         weighted, s_made, s_read, own) = (core.sem(s) for s in (
             "turn_done copied picked cb_made cb_out r_made clamped decayed weighed y_made i_made i_read "
             "weighted s_made s_read own").split())
        SC0 = 2 * GH

        def head(ap):
            return ap.rearrange("p (h c) -> p h c", c=SHD)

        def tl(t):
            return slice(t * P, (t + 1) * P)

        def cols(f, t, d, g):
            lo = SC0 + d * SH + g * HG
            return core.scal[:, f, bass.ds(t, 1), lo:lo + HG].rearrange("p a h -> p (a h)")

        def one(f, t, d, h):
            lo = SC0 + d * SH + h
            return core.scal[:, f, bass.ds(t, 1), lo:lo + 1].rearrange("p a h -> p (a h)")

        def xrow(t, g):
            return core.tok_x[:, bass.ds(t, 1), g * BANK:(g + 1) * BANK].rearrange("p a c -> p (a c)")

        def yrow(t, g):
            return core.y_acc[:, bass.ds(t, 1), g * BANK:(g + 1) * BANK].rearrange("p a c -> p (a c)")

        with core.block() as block:

            @block.scalar
            def _(act):
                with act.Fori(0, TILES) as s:
                    act.wait_ge(turn_done, s + 1)
                    act.activation(cbt[:, :, :], core.chan[:, B0:B0 + 4, bass.ds(s * P, P)], ACT.Copy).then_inc(copied, 1)
                    act.activation(cback[:, :, :], core.chan[:, C0:C0 + 2, bass.ds((TILES - 1) * P - s * P, P)],
                                   ACT.Copy).then_inc(copied, 1)
                    act.wait_ge(cb_made, s + 1)
                    act.activation(cb[:, :, :].rearrange("p g t -> p (g t)"), pc[:, 0:SG * P], ACT.Copy).then_inc(cb_out, 1)
                    for q in range(4):
                        for d in range(2):
                            act.wait_ge(clamped, s * 8 + 2 * q + d + 3)
                            act.activation(dec[:, q % 2, d, :], dec[:, q % 2, d, :], ACT.Exp).then_inc(decayed, 1)

            @block.gpsimd
            def _(pool):
                pool.memset(state[:, :, :, :], 0.0).then_inc(picked, 1)
                pool.memset(core.y_acc[:, :, :], 0.0).then_inc(picked, 1)
                with pool.Fori(0, TILES) as s:
                    back = pool.snap((TILES - 1) - s)
                    pool.wait_ge(turn_done, s + 1)
                    pool.tensor_copy(gs[:, :], core.scal[:, F_G, bass.ds(s, 1), SC0:].rearrange("p a h -> p (a h)")).then_inc(picked, 1)
                    for d in range(2):
                        t = s if d == 0 else back
                        pool.tensor_copy(btok[:, d, :], core.tok_b[:, bass.ds(t, 1), :].rearrange("p a c -> p (a c)")).then_inc(picked, 1)
                    for d in range(2):
                        t = s if d == 0 else back
                        for g in range(SG):
                            pool.tensor_tensor(head(xw[:, d, g, :]), head(xrow(t, g)), over(cols(F_DTW, t, d, g), SHD),
                                               ALU.mult).then_inc(weighted, 1)

            @block.tensor
            def _(pe):
                with pe.Fori(0, TILES) as s:
                    pe.wait_ge(copied, s * 2 + 2)
                    pe.wait_ge(picked, s * 3 + 5)
                    for g in range(SG):
                        last = pe.matmul(pc[:, tl(g)], cbt[:, g, :], cbt[:, 2 + g, :], start=True, stop=True)
                    last.then_inc(cb_made, 1)

                    def decays(q):
                        for d in range(2):
                            pe.wait_ge(clamped, s * 8 + 2 * q + d + 1)
                            for j in range(4):
                                c = d * SH + q * 4 + j
                                last = pe.matmul(pr[:, d, tl(j)], gs[:, c:c + 1].to_broadcast([P, P]),
                                                 core.cst[:, TRI0 + d * P:TRI0 + (d + 1) * P], start=True, stop=True)
                            last.then_inc(r_made, 1)

                    def products(q):
                        pe.wait_ge(weighed, s * 4 + q + 1)
                        for j in range(4):
                            h = q * 4 + j
                            last = pe.matmul(pyy[:, q // 2, (h % HG) * SHD:(h % HG + 1) * SHD],
                                             dec[:, q % 2, 0, tl(j)],
                                             core.tok_x[:, bass.ds(s, 1), h * SHD:(h + 1) * SHD].rearrange("p a c -> p (a c)"),
                                             start=True, stop=True)
                        last.then_inc(y_made, 1)

                    decays(0)
                    for q in range(4):
                        if q < 3:
                            decays(q + 1)
                        products(q)
                    for g in range(SG):
                        for d in range(2):
                            n = s * 4 + 2 * g + d
                            pe.wait_ge(i_read, n + 1)
                            pe.matmul(pi[:, :], cbt[:, 2 + g, :] if d == 0 else cback[:, g, :], state[:, d, g, :],
                                      start=True, stop=True).then_inc(i_made, 1)
                            pe.wait_ge(weighted, s * 4 + 2 * d + g + 1)
                            pe.wait_ge(s_read, n + 1)
                            pe.matmul(pst[:, :], btok[:, d, tl(g)], xw[:, d, g, :], start=True, stop=True).then_inc(s_made, 1)

            @block.vector
            def _(dve):
                dve.sem_inc(turn_done, 1)
                dve.sem_inc(clamped, 2)
                dve.sem_inc(i_read, 1)
                dve.sem_inc(s_read, 1)
                PER = 12 + 2 + 8
                backward = dve.alloc_register("backward")
                dve.reg_mov(backward, TILES - 1)
                with dve.Fori(0, TILES) as s:
                    back = dve.snap(backward, min_val=0, max_val=TILES - 1)
                    steps = Steps(dve, own, s * PER)
                    dve.wait_ge(picked, s * 3 + 5)

                    def clamp(q):
                        for d in range(2):
                            dve.wait_ge(r_made, s * 8 + 2 * q + d + 1)
                            if q >= 2:
                                dve.wait_ge(y_made, s * 4 + q - 1)
                            for j in range(4):
                                last = dve.tensor_scalar(dec[:, q % 2, d, tl(j)], pr[:, d, tl(j)], one(F_GC, s, d, q * 4 + j),
                                                         0.0, ALU.subtract, ALU.min)
                            last.then_inc(clamped, 1)

                    def weigh(q):
                        for d in range(2):
                            dve.wait_ge(decayed, s * 8 + 2 * q + d + 1)
                            for j in range(4):
                                last = dve.scalar_tensor_tensor(out=dec[:, q % 2, d, tl(j)], in0=dec[:, q % 2, d, tl(j)],
                                                                scalar=one(F_DT, s, d, q * 4 + j),
                                                                in1=core.cst[:, TRI0 + d * P:TRI0 + (d + 1) * P],
                                                                op0=ALU.mult, op1=ALU.mult)
                            steps.mark(last)
                        steps.wait()
                        steps.mark(dve.tensor_tensor(dec[:, q % 2, 0, :], dec[:, q % 2, 0, :], dec[:, q % 2, 1, :], ALU.add))
                        steps.wait()
                        dve.wait_ge(cb_out, s + 1)
                        dve.tensor_tensor(tiles(dec[:, q % 2, 0, :]), tiles(dec[:, q % 2, 0, :]), each(cb[:, q // 2, :], 4),
                                          ALU.mult).then_inc(weighed, 1)

                    clamp(0)
                    for q in range(4):
                        if q < 3:
                            clamp(q + 1)
                        weigh(q)
                    for g in range(SG):
                        dve.wait_ge(y_made, s * 4 + 2 * g + 2)
                        steps.wait()
                        steps.mark(dve.tensor_tensor(yrow(s, g), yrow(s, g), pyy[:, g, :], ALU.add))
                    for g in range(SG):
                        for d in range(2):
                            n = s * 4 + 2 * g + d
                            t = s if d == 0 else back
                            dve.wait_ge(i_made, n + 1)
                            steps.wait()
                            dve.tensor_tensor(head(part[:, :]), head(pi[:, :]), over(cols(F_EGC, t, d, g), SHD), ALU.mult).then_inc(i_read, 1)
                            dve.wait_ge(i_read, n + 2)
                            steps.mark(dve.tensor_tensor(yrow(t, g), yrow(t, g), part[:, :], ALU.add))
                            steps.mark(dve.tensor_tensor(head(state[:, d, g, :]), head(state[:, d, g, :]),
                                                         over(cols(F_EGL, t, d, g), SHD), ALU.mult))
                            dve.wait_ge(s_made, n + 1)
                            steps.wait()
                            dve.tensor_tensor(state[:, d, g, :], state[:, d, g, :], pst[:, :], ALU.add).then_inc(s_read, 1)
                    steps.wait()
                    dve.wait_ge(s_read, s * 4 + 5)
                    dve.sem_inc(turn_done, 1)
                    dve.reg_sub(backward, backward, 1)
                assert steps.n == PER


def gate_outputs(core, A):
    w_in = A["w_in"][0].rearrange("(k p) n -> p k n", p=P)
    HG = BANK // P
    with ExitStack() as ctx:
        sb = lambda name, *shape: core.sb(ctx, name, [P, *shape])
        w = sb("w", 2, DK, BANK)
        gate = sb("gate", 2, BANK)
        sq = sb("sq", D)
        dx = sb("dx", 2, D)
        drow = sb("drow", SH)
        stat = sb("stat", 3, TILES, GH)
        ystat = sb("ystat", 3, TILES, SG)
        proj = core.ps(ctx, "proj", [P, 2, BANK])
        w_landed = [core.sem("w_landed") for _ in range(2)]
        (row_in, projected, gated, applied, squared, reduced, o_mean, o_root, own, scaled_x, added_x, y_squared,
         y_mean, y_root) = (core.sem(s) for s in (
             "row_in projected gated applied squared reduced o_mean o_root own scaled_x added_x y_squared "
             "y_mean y_root").split())

        def cols(g):
            return slice((g % 2) * BANK, (g % 2 + 1) * BANK)

        with core.block() as block:

            @block.sync
            def _(sp):
                sp.dma_start(drow[:, :], A["ssd_D"].to_broadcast([P, SH])).then_inc(row_in, 16)
                for g in range(4):
                    if g >= 2:
                        sp.wait_ge(projected, (g - 1) * TILES)
                    sp.dma_start(w[:, g % 2, :, :], w_in[:, :, CONV_CH + g * BANK:CONV_CH + (g + 1) * BANK]
                                 ).then_inc(w_landed[g % 2], 16)

            @block.tensor
            def _(pe):
                for g in range(4):
                    pe.wait_ge(w_landed[g % 2], 16 * (g // 2 + 1))
                    for t in range(TILES):
                        n = g * TILES + t
                        if n >= 2:
                            pe.wait_ge(gated, n - 1)
                        for k in range(DK):
                            last = pe.matmul(proj[:, n % 2, :], core.feat[:, k, t * P:(t + 1) * P], w[:, g % 2, k, :],
                                             start=k == 0, stop=k == DK - 1)
                        last.then_inc(projected, 1)

            @block.gpsimd
            def _(pool):
                pool.wait_ge(row_in, 16)
                for t in range(TILES):
                    if t >= 2:
                        pool.wait_ge(added_x, t - 1)
                    pool.tensor_tensor(dx[:, t % 2, :].rearrange("p (h c) -> p h c", c=SHD),
                                       core.tok_x[:, t, :].rearrange("p (h c) -> p h c", c=SHD),
                                       over(drow[:, :], SHD), ALU.mult).then_inc(scaled_x, 1)
                    pool.wait_ge(scaled_x, t + 1)
                    pool.tensor_tensor(core.y_acc[:, t, :], core.y_acc[:, t, :], dx[:, t % 2, :], ALU.add).then_inc(added_x, 1)

            @block.scalar
            def _(act):
                for t in range(TILES):
                    if t:
                        act.wait_ge(reduced, t)
                    act.activation(sq[:, :], core.o_acc[:, t, :], ACT.Square).then_inc(squared, 1)
                act.wait_ge(o_mean, 1)
                act.activation(stat[:, 1, :, :], stat[:, 0, :, :], ACT.Sqrt).then_inc(o_root, 1)
                for n in range(4 * TILES):
                    if n >= 2:
                        act.wait_ge(applied, n - 1)
                    act.wait_ge(projected, n + 1)
                    act.activation(gate[:, n % 2, :], proj[:, n % 2, :], ACT.Silu).then_inc(gated, 1)
                act.wait_ge(applied, 4 * TILES)
                for t in range(TILES):
                    for g in range(SG):
                        if t or g:
                            act.wait_ge(y_squared, t * SG + g)
                        act.activation(sq[:, 0:BANK], core.y_acc[:, t, g * BANK:(g + 1) * BANK], ACT.Square,
                                       accum_out=ystat[:, 0, t, g:g + 1]).then_inc(y_squared, 1)
                act.wait_ge(y_mean, 1)
                act.activation(ystat[:, 1, :, :], ystat[:, 0, :, :], ACT.Sqrt).then_inc(y_root, 1)

            @block.vector
            def _(dve):
                steps = Steps(dve, own)
                for t in range(TILES):
                    dve.wait_ge(squared, t + 1)
                    dve.tensor_reduce(stat[:, 0, t, :], sq[:, :].rearrange("p (h c) -> p h c", c=P), AX.X, ALU.add).then_inc(reduced, 1)
                dve.wait_ge(reduced, TILES)
                dve.tensor_scalar(stat[:, 0, :, :], stat[:, 0, :, :], 1.0 / P, EPS, ALU.mult, ALU.add).then_inc(o_mean, 1)
                dve.wait_ge(o_root, 1)
                steps.mark(dve.reciprocal(stat[:, 2, :, :], stat[:, 1, :, :]))
                steps.wait()
                for g in range(4):
                    for t in range(TILES):
                        n = g * TILES + t
                        dve.wait_ge(gated, n + 1)
                        if g < 2:
                            for j in range(HG):
                                o = core.o_acc[:, t, (g * HG + j) * P:(g * HG + j + 1) * P]
                                last = dve.scalar_tensor_tensor(out=o, in0=o, scalar=stat[:, 2, t, g * HG + j:g * HG + j + 1],
                                                                in1=gate[:, n % 2, j * P:(j + 1) * P], op0=ALU.mult, op1=ALU.mult)
                        else:
                            dve.wait_ge(added_x, t + 1)
                            y = core.y_acc[:, t, cols(g)]
                            last = dve.tensor_tensor(y, y, gate[:, n % 2, :], ALU.mult)
                        last.then_inc(applied, 1)
                dve.wait_ge(y_squared, TILES * SG)
                dve.tensor_scalar(ystat[:, 0, :, :], ystat[:, 0, :, :], 1.0 / BANK, EPS, ALU.mult, ALU.add).then_inc(y_mean, 1)
                dve.wait_ge(y_root, 1)
                steps.mark(dve.reciprocal(ystat[:, 2, :, :], ystat[:, 1, :, :]))
                steps.wait()
                for t in range(TILES):
                    for g in range(SG):
                        y = core.y_acc[:, t, g * BANK:(g + 1) * BANK]
                        dve.tensor_scalar(y, y, ystat[:, 2, t, g:g + 1], None, ALU.mult)


def mixer_output(core, A):
    MK = 2 * DK
    w_out = A["w_out"][0].rearrange("(k p) n -> p k n", p=P)
    with ExitStack() as ctx:
        w = core.sb(ctx, "w", [P, 2, MK, BANK])
        mix = core.chan[:, 0:MK, :]
        turned = core.ps(ctx, "turned", [P, 2, BANK])
        out = core.ps(ctx, "out", [P, TILES, BANK])
        w_landed = [core.sem("w_landed") for _ in range(2)]
        transposed, mixed, out_made, out_read, moved_a, moved_v = (
            core.sem(s) for s in ("transposed", "mixed", "out_made", "out_read", "moved_a", "moved_v"))
        ident = core.cst[:, ID0:ID0 + P]

        def gain(k):
            return core.cols[:, COL_GDN:COL_GDN + 1] if k < DK else core.cols[:, COL_SSD + k - DK:COL_SSD + k - DK + 1]

        with core.block() as block:

            @block.sync
            def _(sp):
                for half in range(2):
                    sp.dma_start(w[:, half, :, :], w_out[:, :, half * BANK:(half + 1) * BANK]).then_inc(w_landed[half], 16)

            @block.tensor
            def _(pe):
                for k in range(MK):
                    if k >= 2:
                        pe.wait_ge(moved_a if k % 2 == 0 else moved_v, k // 2)
                    src = core.o_acc if k < DK else core.y_acc
                    c = (k % DK) * P
                    for t in range(TILES):
                        last = pe.transpose(turned[:, k % 2, t * P:(t + 1) * P], src[:, t, c:c + P], ident)
                    last.then_inc(transposed, 1)
                pe.wait_ge(moved_a, MK // 2)
                pe.wait_ge(moved_v, MK // 2)
                for half in range(2):
                    pe.wait_ge(w_landed[half], 16)
                    for t in range(TILES):
                        if half:
                            pe.wait_ge(out_read, t + 1)
                        for k in range(MK):
                            last = pe.matmul(out[:, t, :], mix[:, k, t * P:(t + 1) * P], w[:, half, k, :],
                                             start=k == 0, stop=k == MK - 1)
                        last.then_inc(out_made, 1)

            @block.scalar
            def _(act):
                for k in range(0, MK, 2):
                    act.wait_ge(transposed, k + 1)
                    act.activation(mix[:, k, :], turned[:, 0, :], ACT.Copy, scale=gain(k)).then_inc(moved_a, 1)

            @block.vector
            def _(dve):
                for k in range(1, MK, 2):
                    dve.wait_ge(transposed, k + 1)
                    dve.tensor_scalar(mix[:, k, :], turned[:, 1, :], gain(k), None, ALU.mult).then_inc(moved_v, 1)
                for half in range(2):
                    for t in range(TILES):
                        dve.wait_ge(out_made, half * TILES + t + 1)
                        h = core.hid[:, t, half * BANK:(half + 1) * BANK]
                        dve.tensor_tensor(h, h, out[:, t, :], ALU.add).then_inc(out_read, 1)


NE, CAP, FF = 16, 2 * SEQ // 16, 512
PAIRS = NE // 2


def expert_choice_route(core, A, picked_t, scatter):
    E2C = core.e_cst
    with ExitStack() as ctx:
        sb = lambda name, *shape: core.sb(ctx, name, [P, *shape])
        wr = sb("wr", DK, NE)
        aff = sb("aff", TILES, NE)
        stat = sb("stat", 3, TILES)
        work, sel, slot = (core.sb(ctx, s, [NE, SEQ]) for s in ("work", "sel", "slot"))
        aff_e = core.sb(ctx, "aff_e", [NE, SEQ])
        top = core.sb(ctx, "top", [NE, 8])
        ones = core.sb(ctx, "ones", [NE, SEQ])
        slot_t = sb("slot_t", TILES, NE)
        hot = sb("hot", TILES, NE * CAP)
        pl = core.ps(ctx, "pl", [P, BANK])
        pt = core.ps(ctx, "pt", [P, BANK])
        px = core.ps(ctx, "px", [P, 2, BANK])
        pb = core.ps(ctx, "pb", [P, 2, 2, BANK])
        landed, p_sem, a_sem, v_sem, x_made, x_out, b_made, b_out, hot_made = (
            core.sem(s) for s in "landed p_sem a_sem v_sem x_made x_out b_made b_out hot_made".split())
        ident = core.cst[:, ID0:ID0 + P]
        logits = pl[:, 0:TILES * NE].rearrange("p (t e) -> p t e", e=NE)
        row = E2C[:, 0:CAP]
        place = E2C[:, CAP:CAP + 1]
        spread = E2C[0:NE, CAP + 1:CAP + 1 + PAIRS * P].rearrange("e (j r) -> e j r", r=P)
        with core.block() as block:

            @block.sync
            def _(sp):
                sp.dma_start(wr[:, :, :], A["w_router"][0].rearrange("(k p) e -> p k e", p=P)).then_inc(landed, 16)

            @block.tensor
            def _(pe):
                pe.wait_ge(landed, 16)
                for t in range(TILES):
                    for k in range(DK):
                        last = pe.matmul(logits[:, t, :], core.feat[:, k, t * P:(t + 1) * P], wr[:, k, :],
                                         start=k == 0, stop=k == DK - 1)
                last.then_inc(p_sem, 1)
                pe.wait_ge(v_sem, 5)
                for t in range(TILES):
                    last = pe.transpose(pt[0:NE, t * P:(t + 1) * P], aff[:, t, :], ident)
                last.then_inc(p_sem, 1)
                pe.wait_ge(v_sem, 6 + 16 + 4)
                for t in range(TILES):
                    last = pe.transpose(pl[:, t * NE:(t + 1) * NE], slot[:, t * P:(t + 1) * P], ident[0:NE, 0:NE])
                last.then_inc(p_sem, 1)
                for j in range(PAIRS):
                    if j >= 2:
                        pe.wait_ge(b_out, j - 1)
                    pe.matmul(pb[:, j % 2, 0, :], spread[:, j, :], slot[:, :], start=True, stop=True)
                    pe.matmul(pb[:, j % 2, 1, :], spread[:, j, :], aff_e[:, :], start=True, stop=True).then_inc(b_made, 1)
                pe.wait_ge(hot_made, TILES)
                for k in range(DK):
                    for half in range(2):
                        if k:
                            pe.wait_ge(x_out, (k - 1) * 2 + half + 1)
                        for t in range(TILES):
                            last = pe.matmul(px[:, half, :], core.tok[:, t, k * P:(k + 1) * P],
                                             hot[:, t, half * BANK:(half + 1) * BANK], start=t == 0, stop=t == TILES - 1)
                        last.then_inc(x_made, 1)

            @block.scalar
            def _(act):
                act.wait_ge(v_sem, 2)
                act.activation(aff[:, :, :], aff[:, :, :], ACT.Exp).then_inc(a_sem, 1)
                for k in range(DK):
                    for half in range(2):
                        act.wait_ge(x_made, k * 2 + half + 1)
                        act.activation(picked_t[:, k, half * BANK:(half + 1) * BANK], px[:, half, :], ACT.Copy,
                                       scale=core.cols[:, COL_NORM2 + k:COL_NORM2 + k + 1]).then_inc(x_out, 1)

            @block.vector
            def _(dve):
                steps = Steps(dve, v_sem)

                def do(instruction):
                    steps.mark(instruction)
                    steps.wait()

                dve.wait_ge(p_sem, 1)
                do(dve.tensor_reduce(stat[:, 0, :], logits, AX.X, ALU.max))
                do(dve.tensor_tensor(aff[:, :, :], logits, over(stat[:, 0, :], NE), ALU.subtract))
                dve.wait_ge(a_sem, 1)
                do(dve.tensor_reduce(stat[:, 1, :], aff[:, :, :], AX.X, ALU.add))
                do(dve.reciprocal(stat[:, 2, :], stat[:, 1, :]))
                do(dve.tensor_tensor(aff[:, :, :], aff[:, :, :], over(stat[:, 2, :], NE), ALU.mult))
                dve.wait_ge(p_sem, 2)
                dve.tensor_copy(aff_e[:, :], pt[0:NE, :])
                do(dve.tensor_copy(work[:, :], pt[0:NE, :]))
                for _ in range(CAP // 8):
                    do(dve.max(top[:, :], work[:, :]))
                    do(dve.match_replace(work[:, :], top[:, :], work[:, :], -1.0))
                dve.memset(ones[:, :], 1.0)
                do(dve.tensor_scalar(sel[:, :], work[:, :], 0.0, None, ALU.is_lt))
                do(dve.tensor_tensor_scan(slot[:, :], ones[:, :], sel[:, :], 0.0, ALU.mult, ALU.add))
                do(dve.tensor_tensor(slot[:, :], slot[:, :], sel[:, :], ALU.mult))
                do(dve.tensor_scalar(slot[:, :], slot[:, :], 1.0, None, ALU.subtract))
                dve.wait_ge(p_sem, 3)
                do(dve.tensor_copy(slot_t[:, :, :], logits))
                for t in range(TILES):
                    dve.tensor_tensor(hot[:, t, :].rearrange("p (e c) -> p e c", c=CAP), over(slot_t[:, t, :], CAP),
                                      each(row, NE), ALU.is_equal).then_inc(hot_made, 1)
                for j in range(PAIRS):
                    dve.wait_ge(b_made, j + 1)
                    do(dve.tensor_scalar(scatter[:, j, :], pb[:, j % 2, 0, :], place, None, ALU.is_equal))
                    dve.tensor_tensor(scatter[:, j, :], scatter[:, j, :], pb[:, j % 2, 1, :], ALU.mult).then_inc(b_out, 1)


def expert_choice_ffn(core, A, picked_t, scatter):
    FB = FF // P
    with ExitStack() as ctx:
        sb = lambda name, *shape: core.sb(ctx, name, [P, *shape])
        wg, wu = (sb(s, 2, DK, FF) for s in ("wg", "wu"))
        wd = sb("wd", 2, FB, D)
        xe = sb("xe", DK, P)
        sc = sb("sc", SEQ)
        act_g = sb("act_g", FF)
        hid_e = sb("hid_e", FF)
        hid_t = sb("hid_t", FB, P)
        ye = sb("ye", D)
        pg, pu, pt = (core.ps(ctx, s, [P, BANK]) for s in ("pg", "pu", "pt"))
        py, po = (core.ps(ctx, s, [P, 2, BANK]) for s in ("py", "po"))
        g_in, u_in, d_in = ([core.sem(s) for _ in range(2)] for s in ("g_in", "u_in", "d_in"))
        names = "x_ready gu_made silu h_made t_made t_out y_made y_out o_made o_read sc_ready own"
        x_ready, gu_made, silu, h_made, t_made, t_out, y_made, y_out, o_made, o_read, sc_ready, own = (
            core.sem(s) for s in names.split())
        ident = core.cst[:, ID0:ID0 + P]

        def weights(name, e, pat):
            return A[name][0, bass.ds(e, 1)].rearrange(pat, p=P)

        with core.block() as block:

            @block.sync
            def _(sp):
                with sp.Fori(0, PAIRS) as j:
                    for e in range(2):
                        sp.wait_ge(gu_made, j * 2 + e + 1)
                        sp.dma_start(wg[:, e, :, :], weights("w_gate", j * 2 + e, "o (k p) n -> p (o k) n")).then_inc(g_in[e], 16)
                        sp.dma_start(wu[:, e, :, :], weights("w_up", j * 2 + e, "o (k p) n -> p (o k) n")).then_inc(u_in[e], 16)
                        sp.wait_ge(y_made, j * 2 + e + 1)
                        sp.dma_start(wd[:, e, :, :], weights("w_down", j * 2 + e, "o (k p) n -> p (o k) n")).then_inc(d_in[e], 16)

            @block.gpsimd
            def _(pool):
                with pool.Fori(0, PAIRS) as j:
                    pool.wait_ge(gu_made, j * 2 + 2)
                    pool.tensor_copy(xe[:, :, :], picked_t[:, :, bass.ds(j * P, P)]).then_inc(x_ready, 1)
                    pool.wait_ge(o_made, j * 8 + 1)
                    pool.tensor_copy(sc[:, :], scatter[:, bass.ds(j, 1), :].rearrange("p a t -> p (a t)")).then_inc(sc_ready, 1)

            @block.tensor
            def _(pe):
                pe.sem_inc(gu_made, 2)
                pe.sem_inc(y_made, 2)
                pe.sem_inc(o_made, 1)
                with pe.Fori(0, PAIRS) as j:
                    pe.wait_ge(x_ready, j + 1)
                    pe.wait_ge(h_made, j + 1)
                    for e in range(2):
                        rows = slice(e * CAP, (e + 1) * CAP)
                        for pp, ws, landed in ((pg, wg, g_in), (pu, wu, u_in)):
                            pe.wait_ge(landed[e], j * 16 + 16)
                            for k in range(DK):
                                last = pe.matmul(pp[rows, :], xe[:, k, rows], ws[:, e, k, :], start=k == 0, stop=k == DK - 1)
                        last.then_inc(gu_made, 1)
                    pe.wait_ge(h_made, j + 2)
                    for f in range(FB):
                        last = pe.transpose(pt[:, f * P:(f + 1) * P], hid_e[:, f * P:(f + 1) * P], ident)
                    last.then_inc(t_made, 1)
                    pe.wait_ge(t_out, j + 1)
                    pe.wait_ge(y_out, j * 2 + 2)
                    for e in range(2):
                        rows = slice(e * CAP, (e + 1) * CAP)
                        pe.wait_ge(d_in[e], j * 16 + 16)
                        for half in range(2):
                            for f in range(FB):
                                last = pe.matmul(py[rows, half, :], hid_t[:, f, rows], wd[:, e, f, half * BANK:(half + 1) * BANK],
                                                 start=f == 0, stop=f == FB - 1)
                        last.then_inc(y_made, 1)
                    pe.wait_ge(sc_ready, j + 1)
                    for half in range(2):
                        pe.wait_ge(y_out, j * 2 + 3 + half)
                        for t in range(TILES):
                            n = half * TILES + t
                            pe.wait_ge(o_read, j * 8 + n + 1)
                            pe.matmul(po[:, n % 2, :], sc[:, t * P:(t + 1) * P], ye[:, half * BANK:(half + 1) * BANK],
                                      start=True, stop=True).then_inc(o_made, 1)

            @block.scalar
            def _(act):
                act.sem_inc(y_out, 2)
                with act.Fori(0, PAIRS) as j:
                    act.wait_ge(gu_made, j * 2 + 4)
                    act.activation(act_g[:, :], pg[:, :], ACT.Silu).then_inc(silu, 1)
                    act.wait_ge(t_made, j + 1)
                    act.activation(hid_t[:, :, :].rearrange("p f c -> p (f c)"), pt[:, :], ACT.Copy).then_inc(t_out, 1)
                    act.wait_ge(y_made, j * 2 + 4)
                    act.wait_ge(o_made, j * 8 + 1)
                    for half in range(2):
                        act.activation(ye[:, half * BANK:(half + 1) * BANK], py[:, half, :], ACT.Copy).then_inc(y_out, 1)

            @block.vector
            def _(dve):
                dve.sem_inc(h_made, 1)
                dve.sem_inc(o_read, 2)
                with dve.Fori(0, PAIRS) as j:
                    dve.wait_ge(silu, j + 1)
                    dve.tensor_tensor(hid_e[:, :], act_g[:, :], pu[:, :], ALU.mult).then_inc(h_made, 1)
                    for half in range(2):
                        for t in range(TILES):
                            n = half * TILES + t
                            dve.wait_ge(o_made, j * 8 + n + 2)
                            h = core.hid[:, t, half * BANK:(half + 1) * BANK]
                            dve.tensor_tensor(h, h, po[:, n % 2, :], ALU.add).then_inc(o_read, 1)


def final_rms(core, A):
    with ExitStack() as ctx:
        g = core.sb(ctx, "g", [P, D])
        sq = core.sb(ctx, "sq", [P, D])
        stat = core.sb(ctx, "stat", [P, 4, TILES])
        landed, squared, stats, root = (core.sem(s) for s in ("landed", "squared", "stats", "root"))
        with core.block() as block:

            @block.sync
            def _(sp):
                sp.dma_start(g[:, :], A["final_norm"].to_broadcast([P, D])).then_inc(landed, 16)

            @block.scalar
            def _(act):
                for t in range(TILES):
                    if t:
                        act.wait_ge(squared, t)
                    act.activation(sq[:, :], core.hid[:, t, :], ACT.Square, accum_out=stat[:, 0, t:t + 1]).then_inc(squared, 1)
                act.wait_ge(stats, 1)
                act.activation(stat[:, 2, :], stat[:, 1, :], ACT.Sqrt).then_inc(root, 1)

            @block.vector
            def _(dve):
                dve.wait_ge(squared, TILES)
                dve.tensor_scalar(stat[:, 1, :], stat[:, 0, :], 1.0 / D, EPS, ALU.mult, ALU.add).then_inc(stats, 1)
                dve.wait_ge(root, 1)
                dve.reciprocal(stat[:, 3, :], stat[:, 2, :]).then_inc(stats, 1)
                dve.wait_ge(stats, 2)
                dve.wait_ge(landed, 16)
                for t in range(TILES):
                    h = core.hid[:, t, :]
                    dve.scalar_tensor_tensor(out=h, in0=h, scalar=stat[:, 3, t:t + 1], in1=g[:, :], op0=ALU.mult, op1=ALU.mult)


def first_block(core, A):
    with ExitStack() as ctx:
        core.feat = core.sb(ctx, "feat", [P, DK, SEQ])
        with ExitStack() as mixer:
            core.chan = core.sb(mixer, "chan", [P, CCH, SEQ])
            core.scal = core.sb(mixer, "scal", [P, PLANES, TILES, NG])
            rms_to_features(core, core.cols[:, COL_NORM1:COL_NORM1 + DK], core.feat)
            conv_projection(core, A)
            token_scalars(core, A)
            core.tok_x = core.sb(mixer, "tok_x", [P, TILES, D])
            with ExitStack() as recurrences:
                core.tok_v = core.sb(recurrences, "tok_v", [P, TILES, D])
                core.tok_b = core.sb(recurrences, "tok_b", [P, TILES, SG * P])
                channels_to_tokens(core)
                rest = core.chan[:, V0:B0, :].rearrange("p c t -> p (c t)")
                half = TILES * D
                core.o_acc = rest[:, 0:half].rearrange("p (t c) -> p t c", t=TILES)
                core.y_acc = rest[:, half:2 * half].rearrange("p (t c) -> p t c", t=TILES)
                normalize_qk(core)
                gated_delta(core, A)
                ssd(core)
            gate_outputs(core, A)
            mixer_output(core, A)
        with ExitStack() as moe:
            picked_t = core.sb(moe, "picked_t", [P, DK, NE * CAP])
            scatter = core.sb(moe, "scatter", [P, PAIRS, SEQ])
            with ExitStack() as routing:
                core.tok = core.sb(routing, "tok", [P, TILES, D])
                core.e_cst = core.sb(routing, "e_cst", [P, CAP + 1 + PAIRS * P])
                rms_to_features(core, core.cols[:, COL_NORM2:COL_NORM2 + DK], core.feat, tok=core.tok)
                load_route_constants(core, A)
                expert_choice_route(core, A, picked_t, scatter)
            expert_choice_ffn(core, A, picked_t, scatter)
    final_rms(core, A)


def load_route_constants(core, A):
    landed = core.sem("landed")
    with core.block() as block:

        @block.sync
        def _(sp):
            sp.dma_start(core.e_cst[:, :], A["route_shapes"]).then_inc(landed, 16)
            sp.wait_ge(landed, 16)


def route_constants():
    r = np.arange(P)
    spread = np.zeros((P, PAIRS, P), np.float32)
    for j in range(PAIRS):
        spread[2 * j, j, :CAP] = 1
        spread[2 * j + 1, j, CAP:] = 1
    return np.concatenate([np.tile(np.arange(CAP), (P, 1)), (r % CAP)[:, None], spread.reshape(P, -1)], axis=1)


META, NTOK = 16, SEQ + 16
HALF = NTOK // 2
LAYERS = 2
QH, KVH, HD, CC, CW = 8, 2, 64, 512, 31
CCK = CC // P
BUCKETS, MAX_DIST, WINDOW = 32, 128, 128
MASKED = -1.0e30
ALPHA = (2 * LAYERS) ** 0.25
LN_EPS = 1e-5
DFF, NX, DX = 2816, 8, 1408
FC, XC = DFF // P, DX // P
GROUPS = [(0, 4), (4, 4), (8, 4), (12, 3), (15, 4), (19, 4), (23, 4), (27, 4)]
PROJ_CHUNKS = 31
C2L = CCK * (CW + 3)
ROWS = [(t, P) for t in range(TILES)] + [(TILES, META)]
BAND, METAD = 2 * P + WINDOW - 1, P + META + META - 1
NDIST = BAND + METAD + META


def row_cols(t):
    return slice(META + t * P, META + (t + 1) * P) if t < TILES else slice(0, META)


def bucket_constants():
    def bucket(n):
        exact = BUCKETS // 2
        nf = np.float32(max(n, 1))
        large = exact + int(np.float32(np.log(nf / np.float32(exact))) / np.float32(np.log(MAX_DIST / exact)) * np.float32(BUCKETS - exact))
        return n if n < exact else min(large, BUCKETS - 1)

    hot = np.zeros((BUCKETS + 1, NDIST), np.float32)
    for j in range(BAND):
        dist = 2 * P - 1 - j
        hot[bucket(dist) if 0 <= dist < WINDOW else BUCKETS, j] = 1
    for j in range(METAD):
        dist = P + META - 1 - j
        hot[bucket(dist) if dist >= 0 else BUCKETS, BAND + j] = 1
    hot[BUCKETS - 1, BAND + METAD:] = 1
    return hot


def bias_tables(core, A, scratch):
    with ExitStack() as ctx:
        hot = core.sb(ctx, "hot", [BUCKETS + 1, NDIST])
        rb = core.sb(ctx, "rb", [BUCKETS + 1, QH])
        line = core.sb(ctx, "line", [QH, NDIST])
        ps = core.ps(ctx, "ps", [P, 2, BANK])
        landed, masked, made, out, stored, tables = (
            core.sem(s) for s in ("landed", "masked", "made", "out", "stored", "tables"))
        nh = NDIST // 2
        with core.block() as block:

            @block.sync
            def _(sp):
                sp.dma_start(hot[:, :], A["bucket_shapes"]).then_inc(landed, 16)
                sp.dma_start(rb[0:BUCKETS, :], A["rel_bias"]).then_inc(landed, 16)
                sp.dma_start(core.sinks[:, :], A["sinks"].to_broadcast([P, LAYERS * QH])).then_inc(landed, 16)
                sp.dma_start(core.cols2[:, :], A["columns2"]).then_inc(landed, 16)
                sp.wait_ge(out, 1)
                sp.dma_start(scratch, line[:, :].unsqueeze(1).to_broadcast([QH, P, NDIST])).then_inc(stored, 16)
                sp.wait_ge(stored, 16)

                def cut(first, rows, shift, n):
                    return bass.AP(tensor=scratch.tensor, offset=first, ap=[[NDIST + shift, rows], [P * NDIST, QH], [1, n]])

                sp.dma_start(core.bias_n[:, :, 0:META], cut(BAND + METAD, P, 0, META)).then_inc(tables, 16)
                sp.dma_start(core.bias_n[:, :, META:], cut(P - 1, P, -1, 2 * P)).then_inc(tables, 16)
                sp.dma_start(core.bias_0[:, :, 0:META], cut(BAND + P - 1, P, -1, META)).then_inc(tables, 16)
                sp.dma_start(core.bias_0[:, :, META:], cut(2 * P - 1, P, -1, P)).then_inc(tables, 16)
                sp.dma_start(core.bias_m[:, :, :], cut(BAND + P + META - 1, META, -1, META)).then_inc(tables, 16)
                sp.wait_ge(tables, 80)
                sp.wait_ge(landed, 64)

            @block.gpsimd
            def _(pool):
                pool.memset(rb[BUCKETS:BUCKETS + 1, :], MASKED).then_inc(masked, 1)

            @block.tensor
            def _(pe):
                pe.wait_ge(landed, 64)
                pe.wait_ge(masked, 1)
                for half in range(2):
                    last = pe.matmul(ps[0:QH, half, 0:nh], rb[:, :], hot[:, half * nh:(half + 1) * nh], start=True, stop=True)
                last.then_inc(made, 1)

            @block.vector
            def _(dve):
                dve.wait_ge(made, 1)
                dve.tensor_copy(line[:, :].rearrange("h (a n) -> h a n", a=2), ps[0:QH, :, 0:nh]).then_inc(out, 1)


def layer_norm(core, A, which, rows, feat=None, result=None):
    with ExitStack() as ctx:
        gb = core.sb(ctx, "gb", [P, 2, D])
        stats = core.sb(ctx, "stats", [P, len(ROWS), 2, 6])
        mv = core.sb(ctx, "mv", [P, len(ROWS), 2])
        rt = core.sb(ctx, "rt", [P, len(ROWS), 2])
        turned = core.ps(ctx, "turned", [P, 2, 2, BANK])
        landed, own, var, root, normed, transposed, moved, stored = (
            core.sem(s) for s in ("landed", "own", "var", "root", "normed", "transposed", "moved", "stored"))
        ident = core.cst[:, ID0:ID0 + P]
        with core.block() as block:

            @block.sync
            def _(sp):
                sp.dma_start(gb[:, :, :].rearrange("p a d -> p (a d)"),
                             A["norm_rows"][which:which + 1, :].to_broadcast([P, 2 * D])).then_inc(landed, 16)
                if "meta" in A and which == 0:
                    sp.dma_start(core.hid[0:META, TILES, :], A["meta"]).then_inc(landed, 16)
                if result is not None:
                    for n, (t, r) in enumerate(rows):
                        sp.wait_ge(normed, n + 1)
                        sp.dma_start(result[t * P:(t + 1) * P, :], core.hid[:, t, :]).then_inc(stored, 16)
                    sp.wait_ge(stored, 16 * len(rows))

            @block.vector
            def _(dve):
                steps = Steps(dve, own)
                for n, (t, r) in enumerate(rows):
                    if t == TILES and which == 0:
                        dve.wait_ge(landed, 32)
                    for a in range(2):
                        steps.mark(dve.bn_stats(stats[0:r, t, a, :], core.hid[0:r, t, a * BANK:(a + 1) * BANK]))
                for n, (t, r) in enumerate(rows):
                    steps.wait()
                    steps.mark(dve.bn_aggr(mv[0:r, t, :], stats[0:r, t, :, :].rearrange("p a s -> p (a s)")))
                steps.wait()
                for n, (t, r) in enumerate(rows):
                    dve.tensor_scalar(rt[0:r, t, 0:1], mv[0:r, t, 1:2], LN_EPS, None, ALU.add).then_inc(var, 1)
                dve.wait_ge(landed, 32 if which == 0 else 16)
                for n, (t, r) in enumerate(rows):
                    h = core.hid[0:r, t, :]
                    dve.wait_ge(root, n + 1)
                    steps.mark(dve.reciprocal(rt[0:r, t, 1:2], rt[0:r, t, 1:2]))
                    steps.mark(dve.scalar_tensor_tensor(out=h, in0=h, scalar=mv[0:r, t, 0:1], in1=gb[0:r, 0, :],
                                                        op0=ALU.subtract, op1=ALU.mult))
                    steps.wait()
                    dve.scalar_tensor_tensor(out=h, in0=h, scalar=rt[0:r, t, 1:2], in1=gb[0:r, 1, :],
                                             op0=ALU.mult, op1=ALU.add).then_inc(normed, 1)

            @block.scalar
            def _(act):
                for n, (t, r) in enumerate(rows):
                    act.wait_ge(var, n + 1)
                    act.activation(rt[0:r, t, 1:2], rt[0:r, t, 0:1], ACT.Sqrt).then_inc(root, 1)
                if feat is not None:
                    for n, (t, r) in enumerate(rows):
                        act.wait_ge(transposed, n + 1)
                        c = row_cols(t)
                        for a in range(2):
                            last = act.activation(feat[:, a * 4:(a + 1) * 4, c],
                                                  turned[:, n % 2, a, 0:4 * r].rearrange("p (k t) -> p k t", k=4), ACT.Copy)
                        last.then_inc(moved, 1)

            @block.tensor
            def _(pe):
                if feat is not None:
                    for n, (t, r) in enumerate(rows):
                        pe.wait_ge(normed, n + 1)
                        if n >= 2:
                            pe.wait_ge(moved, n - 1)
                        for k in range(DK):
                            last = pe.transpose(turned[:, n % 2, k // 4, (k % 4) * r:(k % 4 + 1) * r],
                                                core.hid[0:r, t, k * P:(k + 1) * P], ident[0:r, 0:r])
                        last.then_inc(transposed, 1)


def project_layer(core, A, i):
    w2 = A["w_in_2"]
    NF = PROJ_CHUNKS - 1
    with ExitStack() as ctx:
        sb = lambda name, *shape: core.sb(ctx, name, [P, *shape])
        w = sb("w", 2, 4, DK * P)
        val = sb("val", CCK, NTOK)
        glu = sb("glu", CCK, NTOK + CW - 1)
        proj = core.ps(ctx, "proj", [P, 2, 2, BANK])
        pv = core.ps(ctx, "pv", [P, 2, BANK])
        w_landed = [core.sem("w_landed") for _ in range(2)]
        w_used, projected, taken, v_made, gated, own, padded = (
            core.sem(s) for s in ("w_used", "projected", "taken", "v_made", "gated", "own", "padded"))
        tap0 = i * C2L
        first_gates = GROUPS[4][0] - 1

        def tap(c, j):
            return core.cols2[:, bass.ds(c * (CW + 3) + (tap0 + j), 1)]

        def halves(ap):
            return ap.rearrange("p (a n) -> p a n", a=2)

        with core.block() as block:

            @block.sync
            def _(sp):
                def load(g, b, c0, n):
                    sp.wait_ge(w_used, g + 1)
                    sp.dma_start(w[:, b, 0:n, :], w2[i, bass.ds(c0, n)].rearrange("c p x -> p c x")).then_inc(w_landed[b], 16)

                for g in range(4):
                    load(g, g % 2, *GROUPS[g])
                with sp.Fori(0, 2) as r:
                    for b in range(2):
                        load(r * 2 + (4 + b), b, r * 8 + (15 + 4 * b), 4)

            @block.gpsimd
            def _(pool):
                pool.memset(glu[:, :, 0:CW - 1], 0.0).then_inc(padded, 1)

            @block.tensor
            def _(pe):
                pe.sem_inc(w_used, 2)

                def chunk(n, slot, b, c):
                    pe.wait_ge(taken, n + 1)
                    for half in range(2):
                        for k in range(DK):
                            last = pe.matmul(proj[:, slot, half, 0:HALF], w[:, b, c, k * P:(k + 1) * P],
                                             core.feat[:, k, half * HALF:(half + 1) * HALF], start=k == 0, stop=k == DK - 1)
                    last.then_inc(projected, 1)

                n = 0
                for g in range(4):
                    pe.wait_ge(w_landed[g % 2], 16 * (g // 2 + 1))
                    for c in range(4 if g < 3 else 2):
                        chunk(n, n % 2, g % 2, c)
                        n += 1
                    if g < 3:
                        pe.wait_ge(projected, n)
                        pe.sem_inc(w_used, 1)
                for t, r in ROWS:
                    for k in range(DK):
                        last = pe.matmul(pv[0:r, t // 4, (t % 4) * P:(t % 4 + 1) * P], core.feat[:, k, row_cols(t)],
                                         w[:, 1, 2, k * P:(k + 1) * P], start=k == 0, stop=k == DK - 1)
                last.then_inc(v_made, 1)
                pe.wait_ge(v_made, 1)
                pe.sem_inc(w_used, 1)
                with pe.Fori(0, 2) as r:
                    for b in range(2):
                        pe.wait_ge(w_landed[b], r * 16 + 48)
                        for c in range(4):
                            chunk(r * 8 + (first_gates + 4 * b + c), c % 2, b, c)
                        pe.wait_ge(projected, r * 8 + (first_gates + 4 * b + 4))
                        pe.sem_inc(w_used, 1)

            @block.scalar
            def _(act):
                act.sem_inc(taken, 2)
                act.wait_ge(padded, 1)
                for n in range(first_gates):
                    act.wait_ge(projected, n + 1)
                    src = proj[:, n % 2, :, 0:HALF]
                    if n < 4:
                        dst, f = val[:, n, :], ACT.Copy
                    elif n < 8:
                        dst, f = glu[:, n - 4, CW - 1:], ACT.Sigmoid
                    elif n < 12:
                        dst, f = core.q_t[:, n - 8, :], ACT.Copy
                    else:
                        dst, f = core.k_t[:, n - 12, :], ACT.Copy
                    act.activation(halves(dst), src, f).then_inc(taken, 1)
                act.wait_ge(v_made, 1)
                act.activation(core.v_tok[:, 0:4, :].rearrange("p t c -> p (t c)"), pv[:, 0, :], ACT.Copy)
                act.activation(core.v_tok[0:META, 4, :], pv[0:META, 1, 0:P], ACT.Copy)
                with act.Fori(0, 8) as r:
                    for c in range(2):
                        act.wait_ge(projected, r * 2 + (first_gates + c + 1))
                        act.activation(halves(core.gates[:, bass.ds(r * 2 + c, 1), :].rearrange("p a n -> p (a n)")),
                                       proj[:, c, :, 0:HALF], ACT.Sigmoid).then_inc(taken, 1)

            @block.vector
            def _(dve):
                for c in range(CCK):
                    dve.wait_ge(taken, 2 + 4 + c + 1)
                    g = glu[:, c, CW - 1:]
                    dve.tensor_tensor(g, g, val[:, c, :], ALU.mult).then_inc(gated, 1)
                dve.wait_ge(gated, CCK)
                with dve.Fori(0, CCK) as c:
                    src = glu[:, bass.ds(c, 1), :].rearrange("p a n -> p (a n)")
                    out = core.conv[:, bass.ds(c, 1), :].rearrange("p a n -> p (a n)")
                    steps = Steps(dve, own, c * CW)
                    steps.mark(dve.tensor_scalar(out, src[:, 0:NTOK], tap(c, 0), tap(c, CW), ALU.mult, ALU.add))
                    for j in range(1, CW):
                        steps.wait()
                        steps.mark(dve.scalar_tensor_tensor(out=out, in0=src[:, j:j + NTOK], scalar=tap(c, j), in1=out,
                                                            op0=ALU.mult, op1=ALU.add))


def attention(core, i):
    units = []
    for hk in range(KVH):
        units.append((hk, META, 0, [(0, META, TILES)], core.bias_m))
    for n in range(TILES):
        for hk in range(KVH):
            keys = [(0, META, TILES)] + ([(META + (n - 1) * P, P, n - 1)] if n else []) + [(META + n * P, P, n)]
            units.append((hk, P, META + n * P, keys, core.bias_n if n else core.bias_0))
    G = QH // KVH
    WMAX = META + 2 * P
    scale = HD ** -0.5
    with ExitStack() as ctx:
        sb = lambda name, *shape: core.sb(ctx, name, [P, *shape])
        s = sb("s", 2, G, WMAX)
        pt = sb("pt", 3, G * P)
        st = sb("st", 2, 6, G)
        ps = core.ps(ctx, "ps", [P, G, BANK])
        ptr = core.ps(ctx, "ptr", [P, 2, BANK])
        po = core.ps(ctx, "po", [P, BANK])
        (s_made, s_read, own, maxed, exped, sunk, inv, scaled, t_made, t_out, o_made, o_out) = (
            core.sem(x) for x in "s_made s_read own maxed exped sunk inv scaled t_made t_out o_made o_out".split())
        ident = core.cst[:, ID0:ID0 + P]
        with core.block() as block:

            @block.tensor
            def _(pe):
                def scores(u):
                    hk, nq, q0, keys, _ = units[u]
                    if u:
                        pe.wait_ge(s_read, u)
                    lo, width = keys[-1][0] + keys[-1][1], sum(k[1] for k in keys[1:])
                    for j in range(G):
                        h = hk * G + j
                        rows = slice((h % 2) * HD, (h % 2 + 1) * HD)
                        q = core.q_t[rows, h // 2, q0:q0 + nq]
                        last = pe.matmul(ps[0:nq, j, 0:META], q, core.k_t[rows, hk, 0:META], start=True, stop=True)
                        if width:
                            last = pe.matmul(ps[0:nq, j, META:META + width], q, core.k_t[rows, hk, lo - width:lo],
                                             start=True, stop=True)
                    last.then_inc(s_made, 1)

                moves = 0
                scores(0)
                for u, (hk, nq, q0, keys, _) in enumerate(units):
                    if u + 1 < len(units):
                        scores(u + 1)
                    pe.wait_ge(scaled, u + 1)
                    at = 0
                    for m, (k0, nk, _) in enumerate(keys):
                        if moves >= 2:
                            pe.wait_ge(t_out, moves - 1)
                        for j in range(G):
                            last = pe.transpose(ptr[0:nk, moves % 2, j * nq:(j + 1) * nq], s[0:nq, u % 2, j, at:at + nk],
                                                ident[0:nq, 0:nq])
                        last.then_inc(t_made, 1)
                        moves += 1
                        at += nk
                    pe.wait_ge(t_out, moves)
                    if u:
                        pe.wait_ge(o_out, u)
                    for par in range(2):
                        for m, (k0, nk, vt) in enumerate(keys):
                            heads = pt[0:nk, m, 0:G * nq].rearrange("p (c r q) -> p c r q", r=2, q=nq)[:, :, par, :]
                            last = pe.matmul(po[par * HD:(par + 1) * HD, 0:2 * nq], core.v_tok[0:nk, vt, hk * HD:(hk + 1) * HD],
                                             heads, start=m == 0, stop=m == len(keys) - 1)
                    last.then_inc(o_made, 1)

            @block.vector
            def _(dve):
                steps = Steps(dve, own)
                for u, (hk, nq, q0, keys, bias) in enumerate(units):
                    width = sum(k[1] for k in keys)
                    x = st[0:nq, u % 2]
                    dve.wait_ge(s_made, u + 1)
                    if u >= 2:
                        dve.wait_ge(t_made, sum(len(v[3]) for v in units[:u - 1]))
                    for j in range(G):
                        last = dve.scalar_tensor_tensor(out=s[0:nq, u % 2, j, 0:width], in0=ps[0:nq, j, 0:width], scalar=scale,
                                                        in1=bias[0:nq, hk * G + j, 0:width], op0=ALU.mult, op1=ALU.add)
                    last.then_inc(s_read, 1)
                    dve.wait_ge(s_read, u + 1)
                    sink = core.sinks[0:nq, i * QH + hk * G:i * QH + (hk + 1) * G]
                    steps.mark(dve.tensor_reduce(x[:, 0, :], s[0:nq, u % 2, :, 0:width], AX.X, ALU.max))
                    steps.wait()
                    steps.mark(dve.tensor_tensor(x[:, 0, :], x[:, 0, :], sink, ALU.max))
                    steps.wait()
                    dve.tensor_tensor(x[:, 1, :], sink, x[:, 0, :], ALU.subtract)
                    dve.tensor_scalar(x[:, 2, :], x[:, 0, :], -1.0, None, ALU.mult).then_inc(maxed, 1)
                    dve.wait_ge(exped, u + 1)
                    steps.mark(dve.tensor_tensor(x[:, 4, :], x[:, 3, :], x[:, 1, :], ALU.add))
                    steps.wait()
                    dve.reciprocal(x[:, 5, :], x[:, 4, :]).then_inc(inv, 1)

            @block.scalar
            def _(act):
                moves = 0

                def soft(u):
                    hk, nq, q0, keys, _ = units[u]
                    width = sum(k[1] for k in keys)
                    x = st[0:nq, u % 2]
                    act.wait_ge(maxed, u + 1)
                    for j in range(G):
                        act.activation(s[0:nq, u % 2, j, 0:width], s[0:nq, u % 2, j, 0:width], ACT.Exp,
                                       bias=x[:, 2, j:j + 1], accum_out=x[:, 3, j:j + 1])
                    act.activation(x[:, 1, :], x[:, 1, :], ACT.Exp).then_inc(exped, 1)

                soft(0)
                for u, (hk, nq, q0, keys, _) in enumerate(units):
                    if u + 1 < len(units):
                        soft(u + 1)
                    for m, (k0, nk, _) in enumerate(keys):
                        act.wait_ge(t_made, moves + 1)
                        if u:
                            act.wait_ge(o_made, u)
                        act.activation(pt[0:nk, m, 0:G * nq], ptr[0:nk, moves % 2, 0:G * nq], ACT.Copy).then_inc(t_out, 1)
                        moves += 1
                    act.wait_ge(o_made, u + 1)
                    act.activation(core.attn[:, hk * 2:hk * 2 + 2, q0:q0 + nq],
                                   po[:, 0:2 * nq].rearrange("p (c q) -> p c q", c=2), ACT.Copy).then_inc(o_out, 1)

            @block.gpsimd
            def _(pool):
                for u, (hk, nq, q0, keys, _) in enumerate(units):
                    width = sum(k[1] for k in keys)
                    pool.wait_ge(inv, u + 1)
                    v = s[0:nq, u % 2, :, 0:width]
                    pool.tensor_tensor(v, v, over(st[0:nq, u % 2, 5, :], width), ALU.mult).then_inc(scaled, 1)


def mix_layer(core, A, i):
    with ExitStack() as ctx:
        sb = lambda name, *shape: core.sb(ctx, name, [P, *shape])
        wp = sb("wp", DK, 2, CCK, P)
        wo = sb("wo", DK, D)
        sq = sb("sq", CCK, NTOK)
        rt = sb("rt", NTOK)
        mixed = core.feat
        ya = sb("ya", 2, NTOK)
        yc = sb("yc", 2, NTOK)
        pp = core.ps(ctx, "pp", [P, 2, 2, 2, BANK])
        wp_in, wo_in, summed, centred, squared, rooted, own, normed, silu, made, gated_a, gated_c, added, out_made, out_read = (
            core.sem(x) for x in ("wp_in wo_in summed centred squared rooted own normed silu made gated_a gated_c added "
                                  "out_made out_read").split())
        ones = core.cst[:, ONE0:ONE0 + P]
        eps = core.cols2[:, LAYERS * C2L:LAYERS * C2L + 1]

        def halves(ap):
            return ap.rearrange("p (a n) -> p a n", a=2)

        def param(c, j):
            o = i * C2L + c * (CW + 3) + CW + 1 + j
            return core.cols2[:, o:o + 1]

        outs = [(half, t, r) for half in range(2) for t, r in ROWS]
        with core.block() as block:

            @block.sync
            def _(sp):
                sp.dma_start(wp[:, :, :, :, :].rearrange("p m a c x -> p m (a c x)"),
                             A["w_mix_2"][i].rearrange("m p x -> p m x")).then_inc(wp_in, 16)
                sp.dma_start(wo[:, :, :], A["w_out_2"][i].rearrange("(k p) n -> p k n", p=P)).then_inc(wo_in, 16)

            @block.tensor
            def _(pe):
                for stage, src in enumerate((core.conv, sq)):
                    if stage:
                        pe.wait_ge(squared, CCK)
                    for half in range(2):
                        for c in range(CCK):
                            last = pe.matmul(pp[:, stage, 0, half, 0:HALF], ones, src[:, c, half * HALF:(half + 1) * HALF],
                                             start=c == 0, stop=c == CCK - 1)
                    last.then_inc(summed, 1)
                pe.wait_ge(wp_in, 16)
                pe.wait_ge(silu, CCK)
                for m in range(DK):
                    if m >= 2:
                        pe.wait_ge(gated_c, m - 1)
                    for a, src in enumerate((core.attn, core.conv)):
                        for half in range(2):
                            for c in range(CCK):
                                last = pe.matmul(pp[:, m % 2, a, half, 0:HALF], wp[:, m, a, c, :],
                                                 src[:, c, half * HALF:(half + 1) * HALF], start=c == 0, stop=c == CCK - 1)
                    last.then_inc(made, 1)
                pe.wait_ge(wo_in, 16)
                pe.wait_ge(added, DK)
                for n, (half, t, r) in enumerate(outs):
                    if n >= 4:
                        pe.wait_ge(out_read, n - 3)
                    for k in range(DK):
                        last = pe.matmul(pp[0:r, n % 2, n // 2 % 2, 0, :], mixed[:, k, row_cols(t)],
                                         wo[:, k, half * BANK:(half + 1) * BANK], start=k == 0, stop=k == DK - 1)
                    last.then_inc(out_made, 1)

            @block.scalar
            def _(act):
                for c in range(CCK):
                    act.wait_ge(centred, c + 1)
                    act.activation(sq[:, c, :], core.conv[:, c, :], ACT.Square).then_inc(squared, 1)
                act.wait_ge(summed, 2)
                act.activation(halves(rt[:, :]), pp[:, 1, 0, :, 0:HALF], ACT.Sqrt, scale=1.0 / CC, bias=eps).then_inc(rooted, 1)
                for c in range(CCK):
                    act.wait_ge(normed, c + 1)
                    act.activation(core.conv[:, c, :], core.conv[:, c, :], ACT.Silu, scale=param(c, 0), bias=param(c, 1)
                                   ).then_inc(silu, 1)

            @block.vector
            def _(dve):
                dve.wait_ge(summed, 1)
                for c in range(CCK):
                    x = halves(core.conv[:, c, :])
                    dve.scalar_tensor_tensor(out=x, in0=pp[:, 0, 0, :, 0:HALF], scalar=-1.0 / CC, in1=x,
                                             op0=ALU.mult, op1=ALU.add).then_inc(centred, 1)
                dve.wait_ge(rooted, 1)
                dve.reciprocal(rt[:, :], rt[:, :]).then_inc(own, 1)
                dve.wait_ge(own, 1)
                for c in range(CCK):
                    dve.tensor_tensor(core.conv[:, c, :], core.conv[:, c, :], rt[:, :], ALU.mult).then_inc(normed, 1)
                for m in range(DK):
                    dve.wait_ge(made, m + 1)
                    if m >= 2:
                        dve.wait_ge(added, m - 1)
                    dve.tensor_tensor(halves(ya[:, m % 2, :]), pp[:, m % 2, 0, :, 0:HALF], halves(core.gates[:, m, :]),
                                      ALU.mult).then_inc(gated_a, 1)
                    dve.tensor_tensor(halves(yc[:, m % 2, :]), pp[:, m % 2, 1, :, 0:HALF], halves(core.gates[:, DK + m, :]),
                                      ALU.mult).then_inc(gated_c, 1)
                for n, (half, t, r) in enumerate(outs):
                    dve.wait_ge(out_made, n + 1)
                    h = core.hid[0:r, t, half * BANK:(half + 1) * BANK]
                    dve.scalar_tensor_tensor(out=h, in0=h, scalar=ALPHA, in1=pp[0:r, n % 2, n // 2 % 2, 0, :],
                                             op0=ALU.mult, op1=ALU.add).then_inc(out_read, 1)

            @block.gpsimd
            def _(pool):
                for m in range(DK):
                    pool.wait_ge(gated_c, m + 1)
                    pool.tensor_tensor(mixed[:, m, :], ya[:, m % 2, :], yc[:, m % 2, :], ALU.add).then_inc(added, 1)


def dense_ffn(core, A):
    with ExitStack() as ctx:
        sb = lambda name, *shape: core.sb(ctx, name, [P, *shape])
        w = sb("w", 2, 2, DK * P)
        wd = sb("wd", 2, FC, BANK)
        hm = sb("hm", FC, NTOK)
        sg = sb("sg", 2, NTOK)
        w_in = [core.sem("w_in") for _ in range(2)]
        wd_in = [core.sem("wd_in") for _ in range(2)]
        made, silu, taken, down, out = (core.sem(x) for x in "made silu taken down out".split())

        def halves(ap):
            return ap.rearrange("p (a n) -> p a n", a=2)

        with ExitStack() as up:
            pp = core.ps(up, "pp", [P, 2, 2, 2, BANK])
            with core.block() as block:

                @block.sync
                def _(sp):
                    with sp.Fori(0, FC // 2) as r:
                        for b in range(2):
                            sp.wait_ge(made, r * 2 + b + 1)
                            sp.dma_start(w[:, b, :, :].rearrange("p a x -> p (a x)"),
                                         A["ffn_up_2"][bass.ds(r * 2 + b, 1)].rearrange("c p x -> p (c x)")).then_inc(w_in[b], 16)
                    wdv = A["ffn_down_2"].rearrange("(f p) n -> p f n", p=P)
                    for half in range(2):
                        sp.dma_start(wd[:, half, :, :], wdv[:, :, half * BANK:(half + 1) * BANK]).then_inc(wd_in[half], 16)

                @block.tensor
                def _(pe):
                    pe.sem_inc(made, 2)
                    with pe.Fori(0, FC // 2) as r:
                        for b in range(2):
                            pe.wait_ge(w_in[b], r * 16 + 16)
                            pe.wait_ge(taken, r * 2 + b + 1)
                            for a in range(2):
                                for half in range(2):
                                    for k in range(DK):
                                        last = pe.matmul(pp[:, b, a, half, 0:HALF], w[:, b, a, k * P:(k + 1) * P],
                                                         core.feat[:, k, half * HALF:(half + 1) * HALF], start=k == 0, stop=k == DK - 1)
                            last.then_inc(made, 1)

                @block.scalar
                def _(act):
                    with act.Fori(0, FC // 2) as r:
                        for b in range(2):
                            act.wait_ge(made, r * 2 + b + 3)
                            act.wait_ge(taken, r * 2 + b + 1)
                            act.activation(halves(sg[:, b, :]), pp[:, b, 0, :, 0:HALF], ACT.Silu).then_inc(silu, 1)

                @block.vector
                def _(dve):
                    dve.sem_inc(taken, 2)
                    with dve.Fori(0, FC // 2) as r:
                        for b in range(2):
                            dve.wait_ge(silu, r * 2 + b + 1)
                            dve.tensor_tensor(halves(hm[:, bass.ds(r * 2 + b, 1), :].rearrange("p a n -> p (a n)")),
                                              halves(sg[:, b, :]), pp[:, b, 1, :, 0:HALF], ALU.mult).then_inc(taken, 1)

        po = core.ps(ctx, "po", [P, len(ROWS), BANK])
        with core.block() as block:

            @block.tensor
            def _(pe):
                for half in range(2):
                    pe.wait_ge(wd_in[half], 16)
                    for n, (t, r) in enumerate(ROWS):
                        if half:
                            pe.wait_ge(out, n + 1)
                        for f in range(FC):
                            last = pe.matmul(po[0:r, t, :], hm[:, f, row_cols(t)], wd[:, half, f, :],
                                             start=f == 0, stop=f == FC - 1)
                        last.then_inc(down, 1)

            @block.vector
            def _(dve):
                for half in range(2):
                    for n, (t, r) in enumerate(ROWS):
                        dve.wait_ge(down, half * len(ROWS) + n + 1)
                        h = core.hid[0:r, t, half * BANK:(half + 1) * BANK]
                        dve.scalar_tensor_tensor(out=h, in0=h, scalar=ALPHA, in1=po[0:r, t, :],
                                                 op0=ALU.mult, op1=ALU.add).then_inc(out, 1)


def top_two(core, A, comb):
    with ExitStack() as ctx:
        sb = lambda name, *shape: core.sb(ctx, name, [P, *shape])
        wr = sb("wr", DK, NX)
        row = sb("row", NX)
        lg = sb("lg", TILES, NX)
        top = sb("top", TILES, 8)
        idx = ctx.enter_context(core.nc.sbuf_tensor("top_idx", [P, TILES, 8], mybir.dt.uint32))
        idf = sb("idf", TILES, 8)
        wt = sb("wt", 3, TILES)
        one = sb("one", 2, TILES, NX)
        pl = core.ps(ctx, "pl", [P, BANK])
        landed, made, own, exped, scaled = (core.sem(x) for x in "landed made own exped scaled".split())
        logits = pl[:, 0:TILES * NX].rearrange("p (t e) -> p t e", e=NX)
        with core.block() as block:

            @block.sync
            def _(sp):
                sp.dma_start(wr[:, :, :], A["router_2"].rearrange("(k p) e -> p k e", p=P)).then_inc(landed, 16)
                sp.dma_start(row[:, :], A["index_row"].to_broadcast([P, NX])).then_inc(landed, 16)

            @block.tensor
            def _(pe):
                pe.wait_ge(landed, 32)
                for t in range(TILES):
                    for k in range(DK):
                        last = pe.matmul(logits[:, t, :], core.feat[:, k, row_cols(t)], wr[:, k, :],
                                         start=k == 0, stop=k == DK - 1)
                last.then_inc(made, 1)

            @block.scalar
            def _(act):
                act.wait_ge(own, 1 + 2 * TILES + 2)
                act.activation(wt[:, 0, :], wt[:, 0, :], ACT.Exp).then_inc(exped, 1)

            @block.gpsimd
            def _(pool):
                for t in range(TILES):
                    h = core.hid[:, t, :]
                    pool.tensor_scalar(h, h, ALPHA, None, ALU.mult).then_inc(scaled, 1)

            @block.vector
            def _(dve):
                steps = Steps(dve, own)

                def do(instruction):
                    steps.mark(instruction)
                    steps.wait()

                dve.wait_ge(made, 1)
                do(dve.tensor_copy(lg[:, :, :], logits))
                for t in range(TILES):
                    do(dve.max(top[:, t, :], lg[:, t, :]))
                    do(dve.max_index(idx[:, t, :], top[:, t, :], lg[:, t, :]))
                do(dve.tensor_copy(idf[:, :, :], idx[:, :, :]))
                do(dve.tensor_tensor(wt[:, 0, :], top[:, :, 1], top[:, :, 0], ALU.subtract))
                dve.wait_ge(exped, 1)
                do(dve.tensor_scalar(wt[:, 1, :], wt[:, 0, :], 1.0, None, ALU.add))
                do(dve.reciprocal(wt[:, 1, :], wt[:, 1, :]))
                do(dve.tensor_tensor(wt[:, 2, :], wt[:, 0, :], wt[:, 1, :], ALU.mult))
                for a in range(2):
                    do(dve.tensor_tensor(one[:, a, :, :], each(row[:, :], TILES), over(idf[:, :, a], NX), ALU.is_equal))
                    do(dve.tensor_tensor(one[:, a, :, :], one[:, a, :, :], over(wt[:, 1 + a, :], NX), ALU.mult))
                dve.wait_ge(scaled, TILES)
                dve.tensor_tensor(comb[:, :, :], one[:, 0, :, :], one[:, 1, :, :], ALU.add)


def expert_ffn(core, A, comb):
    with ExitStack() as ctx:
        sb = lambda name, *shape: core.sb(ctx, name, [P, *shape])
        w = sb("w", XC, 2, DK * P)
        wd = sb("wd", XC, BANK)
        hm = sb("hm", XC, SEQ)
        sg = sb("sg", 2, SEQ)
        ce = sb("ce", TILES)
        pg, pu = (core.ps(ctx, s, [P, 2, BANK]) for s in ("pg", "pu"))
        po = core.ps(ctx, "po", [P, TILES, BANK])
        w_in = [core.sem("w_in") for _ in range(XC)]
        d_in = [core.sem("d_in") for _ in range(XC)]
        made, silu, taken, down, out, picked = (core.sem(x) for x in "made silu taken down out picked".split())
        PER = 2 * TILES
        with core.block() as block:

            @block.sync
            def _(sp):
                with sp.Fori(0, NX) as e:
                    for c in range(XC):
                        sp.wait_ge(made, e * XC + c + 1)
                        sp.dma_start(w[:, c, :, :].rearrange("p a x -> p (a x)"),
                                     A["moe_up_2"][bass.ds(e * XC + c, 1)].rearrange("c p x -> p (c x)")).then_inc(w_in[c], 16)
                    for half in range(2):
                        sp.wait_ge(down, e * PER + half * TILES + TILES)
                        for f in range(XC):
                            sp.dma_start(wd[:, f, :], A["moe_down_2"][bass.ds(e * XC + f, 1), :, half * BANK:(half + 1) * BANK]
                                         .rearrange("c p n -> p (c n)")).then_inc(d_in[f], 16)

            @block.tensor
            def _(pe):
                pe.sem_inc(made, XC)
                pe.sem_inc(down, TILES)
                with pe.Fori(0, NX) as e:
                    for c in range(XC):
                        pe.wait_ge(w_in[c], e * 16 + 16)
                        pe.wait_ge(taken, e * XC + c + 1)
                        for a, pp in enumerate((pg, pu)):
                            for k in range(DK):
                                last = pe.matmul(pp[:, c % 2, :], w[:, c, a, k * P:(k + 1) * P], core.feat[:, k, META:],
                                                 start=k == 0, stop=k == DK - 1)
                        last.then_inc(made, 1)
                    pe.wait_ge(taken, e * XC + XC + 2)
                    for half in range(2):
                        for t in range(TILES):
                            pe.wait_ge(out, e * PER + half * TILES + t + 1)
                            for f in range(XC):
                                if t == 0:
                                    pe.wait_ge(d_in[f], e * 32 + 16 * half + 16)
                                last = pe.matmul(po[:, t, :], hm[:, f, t * P:(t + 1) * P], wd[:, f, :],
                                                 start=f == 0, stop=f == XC - 1)
                            last.then_inc(down, 1)

            @block.scalar
            def _(act):
                with act.Fori(0, NX) as e:
                    for c in range(XC):
                        act.wait_ge(made, e * XC + c + 1 + XC)
                        act.wait_ge(taken, e * XC + c + 1)
                        act.activation(sg[:, c % 2, :], pg[:, c % 2, :], ACT.Silu).then_inc(silu, 1)

            @block.vector
            def _(dve):
                dve.sem_inc(taken, 2)
                dve.sem_inc(out, TILES)
                with dve.Fori(0, NX) as e:
                    for c in range(XC):
                        dve.wait_ge(silu, e * XC + c + 1)
                        dve.tensor_tensor(hm[:, c, :], sg[:, c % 2, :], pu[:, c % 2, :], ALU.mult).then_inc(taken, 1)
                    dve.tensor_copy(ce[:, :], comb[:, :, bass.ds(e, 1)].rearrange("p t o -> p (t o)")).then_inc(picked, 1)
                    for half in range(2):
                        for t in range(TILES):
                            dve.wait_ge(down, e * PER + half * TILES + t + 1 + TILES)
                            dve.wait_ge(picked, e + 1)
                            h = core.hid[:, t, half * BANK:(half + 1) * BANK]
                            dve.scalar_tensor_tensor(out=h, in0=po[:, t, :], scalar=ce[:, t:t + 1], in1=h,
                                                     op0=ALU.mult, op1=ALU.add).then_inc(out, 1)


def second_block(core, A, result):
    with ExitStack() as ctx:
        sb = lambda name, *shape: core.sb(ctx, name, [P, *shape])
        core.feat = sb("feat", DK, NTOK)
        core.cols2 = sb("cols2", LAYERS * C2L + 1)
        core.sinks = sb("sinks", LAYERS * QH)
        with ExitStack() as tables:
            core.bias_n = core.sb(tables, "bias_n", [P, QH, META + 2 * P])
            core.bias_0 = core.sb(tables, "bias_0", [P, QH, META + P])
            core.bias_m = core.sb(tables, "bias_m", [META, QH, META])
            bias_tables(core, A, A["scratch"])
            layer_norm(core, A, 0, ROWS, feat=core.feat)
            for i in range(LAYERS):
                with ExitStack() as layer:
                    lb = lambda name, *shape: core.sb(layer, name, [P, *shape])
                    core.gates, core.conv = lb("gates", 2 * DK, NTOK), lb("conv", CCK, NTOK)
                    core.q_t, core.k_t, core.v_tok = lb("q_t", 4, NTOK), lb("k_t", KVH, NTOK), lb("v_tok", TILES + 1, P)
                    core.attn = lb("attn", CCK, NTOK)
                    project_layer(core, A, i)
                    attention(core, i)
                    mix_layer(core, A, i)
                layer_norm(core, A, 1 + 2 * i, ROWS if i == 0 else ROWS[:TILES], feat=core.feat)
                if i == 0:
                    dense_ffn(core, A)
                    layer_norm(core, A, 2, ROWS, feat=core.feat)
        core.recycle_semaphores()
        comb = sb("comb", TILES, NX)
        top_two(core, A, comb)
        expert_ffn(core, A, comb)
        layer_norm(core, A, 4, ROWS[:TILES], result=result)


def build_program(nc, A, result):
    with ExitStack() as ctx:
        core = Core(nc, ctx)
        core.cst = core.sb(ctx, "cst", [P, NCONST])
        core.cols = core.sb(ctx, "cols", [P, NCOL1])
        core.hid = core.sb(ctx, "hid", [P, TILES + 1, D])
        load_constants(core, A)
        first_block(core, A)
        core.recycle_semaphores()
        second_block(core, A, result)
        core.sem_ctx.close()


def blocks(v):
    return np.asarray(v).reshape(-1, P).T


def chunked(w):
    k, n = w.shape
    return w.reshape(k // P, P, n // P, P).transpose(2, 1, 0, 3).reshape(n // P, P, k)


def lay_out(inputs):
    a = {k: np.asarray(v) for k, v in inputs.items()}
    one = np.ones((P, 1), np.float32)
    conv = np.concatenate([a["conv_w"][0], a["conv_b"]], axis=0)
    w2 = a["w_in_2"]
    q1 = QH * HD
    k1 = q1 + KVH * HD
    v1 = k1 + KVH * HD
    ks = [w2[:, :, q1 + h * HD:q1 + (h + 1) * HD] for h in range(KVH)]
    w2 = np.concatenate([w2[:, :, v1:v1 + 2 * CC], w2[:, :, 0:q1], ks[0], ks[0], ks[1], ks[1], w2[:, :, k1:v1],
                         w2[:, :, v1 + 2 * CC:]], axis=2)
    mix2 = np.stack([np.stack([chunked(a["w_attn_proj_2"][i]), chunked(a["w_conv_proj_2"][i])], axis=2).reshape(DK, P, -1)
                     for i in range(LAYERS)])
    conv2 = np.concatenate([a["conv_dw_2"], a["conv_b_2"][:, None], a["conv_ln_g_2"][:, None], a["conv_ln_b_2"][:, None]],
                           axis=1)
    up2 = np.stack([chunked(a["ffn_w_gate_2"][0]), chunked(a["ffn_w_up_2"][0])], axis=2).reshape(FC, P, -1)
    moe2 = np.concatenate([np.stack([chunked(a["moe_w_gate_2"][0, e]), chunked(a["moe_w_up_2"][0, e])], axis=2).reshape(XC, P, -1)
                           for e in range(NX)])
    out = {
        "x": a["x"],
        "shapes": shape_constants(),
        "level_shapes": level_constants(),
        "columns": np.concatenate([blocks(a["norm1_w"][0]), blocks(a["norm2_w"][0]), blocks(a["ssd_norm_w"][0]),
                                   blocks(a["gdn_norm_w"][0]), one * (EPS * P), one * EPS], axis=1),
        "conv_cols": conv.reshape(TAPS + 1, CCH, P).transpose(2, 1, 0),
        "scal_rows": np.concatenate([a["gdn_dt_bias"].ravel(), a["ssd_dt_bias"].ravel(),
                                     a["gdn_A_log"].ravel(), a["ssd_A_log"].ravel()])[None, :],
        "w_in": a["w_in"],
        "ssd_D": a["ssd_D"],
        "w_out": a["w_out"],
        "w_router": a["w_router"],
        "route_shapes": route_constants(),
        "w_gate": a["w_gate"],
        "w_up": a["w_up"],
        "w_down": a["w_down"],
        "final_norm": a["final_norm_w"][None, :],
        "meta": a["meta_tokens_2"],
        "norm_rows": np.concatenate([a["emb_ln_g_2"][None], a["emb_ln_b_2"][None]] + [
            a[f"ln{j}_{x}_2"][i][None] for i in range(LAYERS) for j in (1, 2) for x in "gb"]).reshape(1 + 2 * LAYERS, 2 * D),
        "bucket_shapes": bucket_constants(),
        "index_row": np.arange(NX)[None, :],
        "rel_bias": a["rel_bias_2"],
        "sinks": a["sinks_2"].reshape(1, -1),
        "columns2": np.concatenate([conv2.reshape(LAYERS, CW + 3, CCK, P).transpose(3, 0, 2, 1).reshape(P, -1), one * LN_EPS], axis=1),
        "w_in_2": np.stack([chunked(w) for w in w2]),
        "w_mix_2": mix2,
        "w_out_2": a["w_out_2"],
        "ffn_up_2": up2,
        "ffn_down_2": a["ffn_w_down_2"][0],
        "router_2": a["router_2"][0],
        "moe_up_2": moe2,
        "moe_down_2": a["moe_w_down_2"][0].reshape(NX * XC, P, D),
    }
    return {k: np.ascontiguousarray(v, dtype=np.float32) for k, v in out.items()}


def kernel(**inputs):
    import concourse.bacc as _bacc
    from concourse.bass_utils import run_bass_kernel_spmd as _run

    nc = _bacc.Bacc("TRN2", target_bir_lowering=False, num_devices=1)
    arrays = lay_out(inputs)
    A = {n: nc.dram_tensor(f"in_{n}", v.shape, F32, kind="ExternalInput").ap() for n, v in arrays.items()}
    A["scratch"] = nc.dram_tensor("bias_lines", (QH, P, NDIST), F32, kind="Internal").ap()
    result = nc.dram_tensor("result", (SEQ, D), F32, kind="ExternalOutput").ap()
    build_program(nc, A, result)
    r = _run(nc, [{f"in_{n}": v for n, v in arrays.items()}], core_ids=[0])
    return r.results[0]["result"].reshape(1, SEQ, D)
```
